# Optimizing a Trainium2 kernel written in Bass

```python
import math
import jax
import jax.numpy as jnp
from jax import lax
import numpy as np

D_MODEL = 1024
BATCH = 1
SEQ = 512
DEPTH = 1

HG_HEADS = 4
HG_DK = 128
HG_DV = 128
HG_K = HG_HEADS * HG_DK
HG_V = HG_HEADS * HG_DV
HG_CHUNK = 64
NSA_HEADS = 8
NSA_KV = 2
NSA_DH = 64
NSA_HPG = NSA_HEADS // NSA_KV
NSA_Q = NSA_HEADS * NSA_DH
NSA_KVW = NSA_KV * NSA_DH
CMP_BLOCK = 32
CMP_STRIDE = 16
CMP_HID = 128
SEL_BLOCK = 64
SEL_TOPK = 8
WINDOW = 512
Q_BLOCK = 128
FORCE_BONUS = 1000.0
REL_BUCKETS = 32
REL_MAX_DIST = 1024
D_FF = 4 * D_MODEL
EPS = 1e-6
NEG_BIG = -1e30

_SPLITS = (HG_K, HG_K, HG_V, HG_V, NSA_Q, NSA_KVW, NSA_KVW, NSA_KVW, NSA_KVW, NSA_KVW, NSA_KVW, 3 * NSA_HEADS, D_MODEL, D_MODEL)
IN_COLS = sum(_SPLITS)

kernel_name = "hybrid_hgrn2_nsa_block"

def rms_norm(x, gain):
    xf = x.astype(jnp.float32)
    xf = xf * lax.rsqrt(jnp.mean(xf * xf, axis=-1, keepdims=True) + EPS)
    return xf.astype(x.dtype) * gain

def rel_bucket(dist):
    max_exact = REL_BUCKETS // 2
    d = jnp.maximum(dist, 0)
    df = jnp.maximum(d, 1).astype(jnp.float32)
    large = max_exact + (jnp.log(df / max_exact) / math.log(REL_MAX_DIST / max_exact) * (REL_BUCKETS - max_exact)).astype(jnp.int32)
    return jnp.where(d < max_exact, d, jnp.minimum(large, REL_BUCKETS - 1))

def masked_softmax(s, valid, axis):
    s = jnp.where(valid, s.astype(jnp.float32), NEG_BIG)
    p = jax.nn.softmax(s, axis=axis)
    return jnp.where(valid, p, 0.0)

def hgrn2_mixer(q, f_logit, i_in, g, lb, out_gain):
    dt = q.dtype
    B, S, _ = q.shape
    nc = S // HG_CHUNK
    z = f_logit.astype(jnp.float32)
    lbf = lb.astype(jnp.float32)
    log_f = jnp.logaddexp(jnp.log(lbf), jnp.log1p(-lbf) + jax.nn.log_sigmoid(z))
    k = (1.0 - lbf) * jax.nn.sigmoid(-z)

    def chunks(t, d):
        return t.astype(jnp.float32).reshape(B, nc, HG_CHUNK, HG_HEADS, d).transpose(1, 0, 3, 2, 4)

    xs = (chunks(q, HG_DK), chunks(k, HG_DK), chunks(log_f, HG_DK), chunks(i_in, HG_DV))
    causal = jnp.tril(jnp.ones((HG_CHUNK, HG_CHUNK), dtype=bool))[:, :, None]

    def step(state, inp):
        qb, kb, gb, vb = inp
        b = jnp.cumsum(gb, axis=2)
        diff = b[:, :, :, None, :] - b[:, :, None, :, :]
        decay = jnp.exp(jnp.where(causal, diff, -jnp.inf))
        scores = jnp.einsum('bhtd,bhsd,bhtsd->bhts', qb, kb, decay)
        o = jnp.einsum('bhtd,bhdv->bhtv', qb * jnp.exp(b), state) + jnp.einsum('bhts,bhsv->bhtv', scores, vb)
        b_last = b[:, :, -1:, :]
        new_state = jnp.exp(b_last[:, :, 0, :, None]) * state + jnp.einsum('bhsd,bhsv->bhdv', kb * jnp.exp(b_last - b), vb)
        return new_state, o

    state0 = jnp.zeros((B, HG_HEADS, HG_DK, HG_DV), jnp.float32)
    _, o = lax.scan(step, state0, xs)
    o = o.transpose(1, 0, 3, 2, 4).reshape(B, S, HG_HEADS, HG_DV)
    o = rms_norm(o, out_gain.astype(jnp.float32)) * jax.nn.silu(g.astype(jnp.float32).reshape(B, S, HG_HEADS, HG_DV))
    return o.reshape(B, S, HG_V).astype(dt)

def nsa_mixer(q, k_c, v_c, k_s, v_s, k_w, v_w, gate_logit, qk_gain, cmp_pos, cmp_w1, cmp_b1, cmp_w2, rel_bias):
    dt = q.dtype
    B, S, _ = q.shape
    G, HPG, DH = NSA_KV, NSA_HPG, NSA_DH
    scale = DH ** -0.5
    q = rms_norm(q.reshape(B, S, G, HPG, DH), qk_gain[0]).transpose(0, 2, 3, 1, 4)
    gates = jax.nn.sigmoid(gate_logit.astype(jnp.float32)).reshape(B, S, G, HPG, 3).transpose(0, 2, 3, 1, 4)

    def heads(t):
        return t.reshape(B, S, G, DH).transpose(0, 2, 1, 3)

    k_s = rms_norm(heads(k_s), qk_gain[2])
    v_s = heads(v_s)
    k_w = rms_norm(heads(k_w), qk_gain[3])
    v_w = heads(v_w)

    n_cmp = (S - CMP_BLOCK) // CMP_STRIDE + 1
    cmp_tok = np.arange(n_cmp)[:, None] * CMP_STRIDE + np.arange(CMP_BLOCK)[None, :]

    def compress(t, j):
        blk = heads(t)[:, :, cmp_tok] + cmp_pos[j]
        blk = blk.reshape(B, G, n_cmp, CMP_BLOCK * DH)
        return jax.nn.gelu(blk @ cmp_w1[j] + cmp_b1[j]) @ cmp_w2[j]

    k_cmp = rms_norm(compress(k_c, 0), qk_gain[1])
    v_cmp = compress(v_c, 1)
    cmp_end = jnp.asarray(cmp_tok[:, -1], jnp.int32)

    n_sel = S // SEL_BLOCK
    sel_start = np.arange(n_sel) * SEL_BLOCK
    overlap = jnp.asarray(((cmp_tok[:, 0][:, None] < sel_start[None, :] + SEL_BLOCK) & (cmp_tok[:, -1][:, None] >= sel_start[None, :])).astype(np.float32))
    sel_start_j = jnp.asarray(sel_start, jnp.int32)
    k_blk = k_s.reshape(B, G, n_sel, SEL_BLOCK, DH)
    v_blk = v_s.reshape(B, G, n_sel, SEL_BLOCK, DH)
    n_top = min(SEL_TOPK, n_sel)
    bi = jnp.arange(B)[:, None, None, None]
    gi = jnp.arange(G)[None, :, None, None]
    g6 = jnp.arange(G)[None, :, None, None, None, None]
    h6 = jnp.arange(HPG)[None, None, :, None, None, None]
    jj = jnp.arange(n_sel, dtype=jnp.int32)

    k_wp = jnp.pad(k_w, ((0, 0), (0, 0), (WINDOW, 0), (0, 0)))
    v_wp = jnp.pad(v_w, ((0, 0), (0, 0), (WINDOW, 0), (0, 0)))
    bias_gh = rel_bias.reshape(REL_BUCKETS, G, HPG).transpose(1, 2, 0)

    def block(qi):
        start = qi * Q_BLOCK
        qb = lax.dynamic_slice_in_dim(q, start, Q_BLOCK, axis=3)
        gb = lax.dynamic_slice_in_dim(gates, start, Q_BLOCK, axis=3)
        t = start + jnp.arange(Q_BLOCK, dtype=jnp.int32)
        dist_c = t[:, None] - cmp_end[None, :]
        s_c = jnp.einsum('bghqd,bgcd->bghqc', qb, k_cmp) * scale + bias_gh[:, :, rel_bucket(dist_c)]
        p_c = masked_softmax(s_c, dist_c >= 0, -1)
        o_c = jnp.einsum('bghqc,bgcd->bghqd', p_c, v_cmp)
        imp = jnp.einsum('bghqc,cj->bgqj', p_c, overlap)
        j_cur = t // SEL_BLOCK
        forced = (jj[None, :] == 0) | (jj[None, :] == j_cur[:, None]) | (jj[None, :] == j_cur[:, None] - 1)
        imp = jnp.where(sel_start_j[None, :] <= t[:, None], imp + FORCE_BONUS * forced, -1.0)
        _, idx = lax.top_k(imp, n_top)
        k_g = k_blk[bi, gi, idx]
        v_g = v_blk[bi, gi, idx]
        pos = idx[..., None] * SEL_BLOCK + jnp.arange(SEL_BLOCK, dtype=jnp.int32)
        dist_s = t[None, None, :, None, None] - pos
        bias_s = bias_gh[g6, h6, rel_bucket(dist_s)[:, :, None]]
        s_s = jnp.einsum('bghqd,bgqnkd->bghqnk', qb, k_g) * scale + bias_s
        p_s = masked_softmax(s_s, (dist_s >= 0)[:, :, None], (-2, -1))
        o_s = jnp.einsum('bghqnk,bgqnkd->bghqd', p_s, v_g)
        kw = lax.dynamic_slice_in_dim(k_wp, start, WINDOW + Q_BLOCK, axis=2)
        vw = lax.dynamic_slice_in_dim(v_wp, start, WINDOW + Q_BLOCK, axis=2)
        key_pos = start - WINDOW + jnp.arange(WINDOW + Q_BLOCK, dtype=jnp.int32)
        dist_w = t[:, None] - key_pos[None, :]
        valid_w = (dist_w >= 0) & (dist_w < WINDOW) & (key_pos[None, :] >= 0)
        s_w = jnp.einsum('bghqd,bgkd->bghqk', qb, kw) * scale + bias_gh[:, :, rel_bucket(dist_w)]
        p_w = masked_softmax(s_w, valid_w, -1)
        o_w = jnp.einsum('bghqk,bgkd->bghqd', p_w, vw)
        return gb[..., 0:1] * o_c + gb[..., 1:2] * o_s + gb[..., 2:3] * o_w

    out = lax.map(block, jnp.arange(S // Q_BLOCK))
    return out.transpose(1, 0, 4, 2, 3, 5).reshape(B, S, NSA_Q).astype(dt)

def setup_inputs(seed: int = 0) -> dict:
    key = jax.random.key(seed)
    ks = jax.random.split(key, 17)
    f32 = jnp.float32

    def nrm(k, shape, scale):
        return jax.random.normal(k, shape, f32) * scale

    def gain(k, shape):
        return 1.0 + 0.02 * jax.random.normal(k, shape, f32)

    return {
        "x": nrm(ks[0], (BATCH, SEQ, D_MODEL), 1.0),
        "rel_bias": nrm(ks[1], (REL_BUCKETS, NSA_HEADS), 0.5),
        "hg_lb_logits": nrm(ks[2], (DEPTH, HG_K), 0.5),
        "norm_mix": gain(ks[3], (DEPTH, D_MODEL)),
        "w_in": nrm(ks[4], (DEPTH, D_MODEL, IN_COLS), D_MODEL ** -0.5),
        "hg_out_gain": gain(ks[5], (DEPTH, HG_DV)),
        "nsa_qk_gain": gain(ks[6], (DEPTH, 4, NSA_DH)),
        "cmp_pos": nrm(ks[7], (DEPTH, 2, CMP_BLOCK, NSA_DH), 0.02),
        "cmp_w1": nrm(ks[8], (DEPTH, 2, CMP_BLOCK * NSA_DH, CMP_HID), (CMP_BLOCK * NSA_DH) ** -0.5),
        "cmp_b1": nrm(ks[9], (DEPTH, 2, CMP_HID), 0.01),
        "cmp_w2": nrm(ks[10], (DEPTH, 2, CMP_HID, NSA_DH), CMP_HID ** -0.5),
        "w_branch_a": nrm(ks[11], (DEPTH, HG_V, D_MODEL), HG_V ** -0.5),
        "w_branch_b": nrm(ks[12], (DEPTH, NSA_Q, D_MODEL), NSA_Q ** -0.5),
        "w_out": nrm(ks[13], (DEPTH, D_MODEL, D_MODEL), D_MODEL ** -0.5),
        "norm_mlp": gain(ks[14], (DEPTH, D_MODEL)),
        "w_up": nrm(ks[15], (DEPTH, D_MODEL, D_FF), D_MODEL ** -0.5),
        "w_down": nrm(ks[16], (DEPTH, D_FF, D_MODEL), 0.5 * D_FF ** -0.5),
    }

def reference(x, rel_bias, hg_lb_logits, norm_mix, w_in, hg_out_gain, nsa_qk_gain, cmp_pos, cmp_w1, cmp_b1, cmp_w2, w_branch_a, w_branch_b, w_out, norm_mlp, w_up, w_down):
    lb_cum = jnp.cumsum(jax.nn.softmax(hg_lb_logits.astype(jnp.float32), axis=0), axis=0)
    lower_bounds = lb_cum - lb_cum[0:1]
    offsets = np.cumsum(_SPLITS)[:-1].tolist()
    for l in range(DEPTH):
        h = rms_norm(x, norm_mix[l])
        (hq, hf, hi, hg, nq, kc, vc, ksl, vsl, kwn, vwn, ngate, gate_a, gate_b) = jnp.split(h @ w_in[l], offsets, axis=-1)
        y_a = hgrn2_mixer(hq, hf, hi, hg, lower_bounds[l], hg_out_gain[l]) @ w_branch_a[l]
        y_b = nsa_mixer(nq, kc, vc, ksl, vsl, kwn, vwn, ngate, nsa_qk_gain[l], cmp_pos[l], cmp_w1[l], cmp_b1[l], cmp_w2[l], rel_bias) @ w_branch_b[l]
        mixed = jax.nn.sigmoid(gate_a) * y_a + jax.nn.sigmoid(gate_b) * y_b
        x = x + mixed @ w_out[l]
        h = rms_norm(x, norm_mlp[l])
        x = x + jnp.square(jax.nn.relu(h @ w_up[l])) @ w_down[l]
    return x


_drawn_inputs = setup_inputs


def setup_inputs(seed=0):
    import zlib

    import numpy as np

    out = dict(_drawn_inputs(seed))
    spreads = {}
    factors = {'norm_mix': 3.583,
     'hg_out_gain': 7.643,
     'nsa_qk_gain': 8.0,
     'cmp_pos': 35.0,
     'cmp_b1': 57.837,
     'norm_mlp': 15.783,
     'rel_bias': 5.58}
    for name, (base, spread) in spreads.items():
        noise = np.random.default_rng([zlib.crc32(name.encode()), seed]).standard_normal(out[name].shape)
        drawn = base * np.exp(spread * noise) if base else spread * noise
        out[name] = jnp.asarray(drawn.astype(out[name].dtype))
    for name, factor in factors.items():
        out[name] = (out[name] * factor).astype(out[name].dtype)
    return out
```

```python
from contextlib import ExitStack

import numpy as np

import concourse.bass as bass
from concourse import mybir

F32 = mybir.dt.float32
F32R = mybir.dt.float32r
U8 = mybir.dt.uint8
ACT = mybir.ActivationFunctionType
ALU = mybir.AluOpType
AX_X = mybir.AxisListType.X

P = 128
D = 1024
S = 512
KT = D // P
ST = S // P
HG = 4
NH = 8
DH = 64
NCMP = 31
FF = 4096
EPS = 1e-6
BIG = 1e30
CW = 1024
NRAW = 4
NSPLIT = 2
LEVELS = [1, 2, 4, 8, 16, 32, 64, 128, 256]
TW = 640

CHUNKS = [f"{a}{h}" for h in range(HG) for a in "fq"] + [f"i{c}" for c in range(4)]
CHUNKS += ["kc", "vc", "ks", "kw", "nq0", "nq1", "nq2", "nq3", "m0", "m1", "m2", "g0", "g1", "g2", "g3"]
CHUNKS += ["c00", "c01", "c10", "c11"]
CHUNKS += [f"{a}{n}" for a in ("ga", "gb") for n in range(KT)]
CHUNKS += [f"ab{n}" for n in range(KT)] + [f"wo{n}" for n in range(KT)]
N_STRAIGHT = len(CHUNKS)
HALVES = 2
UP_T = FF // P // HALVES
N_CHUNKS = N_STRAIGHT + HALVES * (UP_T + KT * UP_T // KT)
AT = {name: n for n, name in enumerate(CHUNKS)}
FIRST = N_CHUNKS % 4 + 4

SMALL = 55
N_CONSTS = 6
MCOLS = 280
NM = [3, 3, 2]


def build_block(nc, xT, w, oh, masks, ident_in, small_in, w2, rel, scratch, skewed, out):
    with ExitStack() as ctx:
        base = (nc.sbuf_base + 31) // 32 * 32

        def at(name, kb, shape, dt=F32):
            return nc.alloc_sbuf_tensor_at(name, shape, dt, offset=base + int(kb * 1024))

        def sem(name):
            return ctx.enter_context(nc.semaphore(name))

        ones = at("ones", 0, [P, P])
        pair_ones = at("pair_ones", 0.5, [P, P])
        ident = at("ident", 1, [P, P])
        mask = at("mask", 1.5, [P, 7 * 256 + 512], U8)
        mask_f = at("mask_f", 190.5, [P, 7 * 64 + P])
        small = at("small", 3.75, [P, 128])
        g_mix, g_mlp = small[:, 0:8], small[:, 8:16]
        g_hg, g_q, g_kc, g_ks, g_kw, b1_k, b1_v = (small[:, n:n + 1] for n in range(16, 23))
        pos_k, pos_v = small[:, 23:39], small[:, 39:55]
        eps = small[:, 64:65]
        hhi = at("hhi", 4.5, [P, KT, S], F32R)
        hlo = at("hlo", 20.5, [P, KT, S], F32R)
        wraw = at("wraw", 36.5, [P, NRAW, CW])
        whi = at("whi", 52.5, [P, NSPLIT, CW], F32R)
        wlo = at("wlo", 60.5, [P, NSPLIT, CW], F32R)
        x0 = at("x0", 68.5, [P, KT, S])
        xsq = at("xsq", 84.5, [P, KT, S])
        hf = at("hf", 100.5, [P, 2, S])
        q_raw = at("q_raw", 68.5, [P, HG, S])
        q_dec = at("q_dec", 76.5, [P, HG, S])
        k_dec = at("k_dec", 84.5, [P, HG, S])
        f = at("f", 92.5, [P, HG, S])
        e = at("e", 100.5, [P, HG, S])
        tot = at("tot", 100.5, [P, HG * S])
        sc = at("sc", 108.5, [P, HG, 10, P])
        v_i = at("v_i", 128.5, [P, ST, S])
        gs = at("gs", 136.5, [P, HG, S])
        oahi = at("oahi", 144.5, [P, HG, S], F32R)
        oalo = at("oalo", 152.5, [P, HG, S], F32R)
        qn = at("qn", 160.5, [P, 4, S])
        ksn = at("ksn", 168.5, [P, S])
        kwn = at("kwn", 170.5, [P, S])
        v_sw = at("v_sw", 172.5, [P, ST, 256])
        kc_raw = at("kc_raw", 176.5, [P, S])
        vc_raw = at("vc_raw", 178.5, [P, S])
        sq = at("sq", 180.5, [P, 2, S])
        rstd = at("rstd", 184.5, [P, 2, S])
        tmp = at("tmp", 188.5, [P, S])
        oblo = at("oblo", 190.5, [P, 4, S], F32R)
        pT = at("pT", 198.5, [P, 3, S])
        cst = at("cst", 204.5, [P, 384])
        gates = at("gates", 68.5, [P, 2, KT, S])
        bias = at("bias", 100.5, [P, NH, S])
        xf = at("xf", 116.5, [P, 16, 2, 32])
        xhi = at("xhi", 120.5, [P, 16, 2, 32], F32R)
        xlo = at("xlo", 124.5, [P, 16, 2, 32], F32R)
        p_ring = at("p_ring", 128.5, [P, 4, S])
        obhi = at("obhi", 136.5, [P, 4, S], F32R)
        o_tok = at("o_tok", 116.5, [P, ST, S])
        vbd = at("vbd", 124.5, [P, 2, 256])
        pc = at("pc", 126.5, [P, 256])
        pcT = at("pcT", 127.5, [P, 2, P])
        x2 = at("x2", 100.5, [P, KT, S])
        uhi = at("uhi", 116.5, [P, UP_T, S], F32R)
        ulo = at("ulo", 148.5, [P, UP_T, S], F32R)
        r_ring = at("r_ring", 72.5, [P, 2, S])
        u_ring = at("u_ring", 76.5, [P, 2, S])
        gate3 = cst[:, 0:96].rearrange("p (t c) -> p t c", t=ST)
        sums = [cst[:, n:n + 16].rearrange("p (b h) -> p b h", b=2) for n in (96, 360)]
        wts = cst[:, 112:128].rearrange("p (b h) -> p b h", b=2)
        mins = cst[:, 128:132]
        mc, sumc, wc, okc = (cst[:, n:n + 8] for n in (136, 144, 152, 160))
        w2_k, w2_v = cst[:, 168:296], cst[:, 296:360]
        relx = at("relx", 198.5, [33, NH])
        ohs = at("ohs", 199.5, [33, TW])
        line = at("line", 202.5, [NH, TW - 128])
        line2 = at("line2", 198.75, [NH, 128])
        hid = at("hid", 180.5, [P, 8, 64])
        gel = at("gel", 182.5, [P, 2, 64])
        kcn = at("kcn", 183, [P, 32])

        bank = [ctx.enter_context(nc.psum_tensor(f"bank{n}", [P, 512], F32)) for n in range(8)]

        w_landed = [sem(f"w_landed{n}") for n in range(NRAW)]
        w_split = sem("w_split")
        w_open = sem("w_open")
        w_hi = sem("w_hi")
        w_used = sem("w_used")
        x_in = [sem("x_in0"), sem("x_in1")]
        consts_in = sem("consts_in")
        bias_line = sem("bias_line")
        line_out = sem("line_out")
        skew_out = sem("skew_out")
        bias_in = sem("bias_in")
        x_again = sem("x_again")
        set_up = sem("set_up")
        free = [sem("bank0_read"), sem("bank1_read")]
        stat_in = sem("stat_in")
        stat_out = sem("stat_out")
        rs_ready = sem("rs_ready")
        rs_used = sem("rs_used")
        act_step = sem("act_step")
        dve_step = sem("dve_step")
        hf_ready, h_hi, h_lo = sem("hf_ready"), sem("h_hi"), sem("h_lo")
        f_exp, q_copied, kq_ready = sem("f_exp"), sem("q_copied"), sem("kq_ready")
        decayed = sem("decayed")
        sc_done = sem("sc_done")
        sc_kept = [sem("sc_kept6"), sem("sc_kept7")]
        tok_copied = sem("tok_copied")
        o_done = sem("o_done")
        o_free = sem("o_free")
        g_sig = sem("g_sig")
        gs_ready = sem("gs_ready")
        raw_copied = sem("raw_copied")
        normed = sem("normed")
        oa_f, oa_hi, oa_lo = sem("oa_f"), sem("oa_hi"), sem("oa_lo")
        xc_f, xc_hi, xc_lo = sem("xc_f"), sem("xc_hi"), sem("xc_lo")
        cexp, csum = sem("cexp"), sem("csum")
        gel_ready, cmp_out, kcn_ready, vbd_ready = (sem(n) for n in ("gel_ready", "cmp_out", "kcn_ready", "vbd_ready"))
        cs_done, cs_shift, cp_ready, cpT_done, cpT_copied, co_done, co_kept = (
            sem(n) for n in ("cs_done", "cs_shift", "cp_ready", "cpT_done", "cpT_copied", "co_done", "co_kept"))
        s_done, s_shift, p_ready, t_done = (sem(n) for n in ("s_done", "s_shift", "p_ready", "t_done"))
        pt_ready = [sem("pt_ready_s"), sem("pt_ready_w")]
        pv_done, ob_read, ot_ready, ot_done, ob_hi, ob_lo = (
            sem(n) for n in ("pv_done", "ob_read", "ot_ready", "ot_done", "ob_hi", "ob_lo"))
        gate_sig = sem("gate_sig")
        mix_f, mix_hi, mix_lo = sem("mix_f"), sem("mix_hi"), sem("mix_lo")
        x2_ready, x2_sq, sq_sum = sem("x2_ready"), sem("x2_sq"), sem("sq_sum")
        relu_d, u_f, u_hi, u_lo = (sem(n) for n in ("relu_d", "u_f", "u_hi", "u_lo"))
        y_ready, y_out = sem("y_ready"), sem("y_out")

        users = []
        for h in range(HG):
            users += [f"f{h}", f"q{h}"]
        users = ["stat_x"] + users + ["kc", "vc", "ks", "kw", "st_ks", "nq0", "st_kw", "nq1", "st_q0", "nq2", "st_q1",
                 "nq3", "st_q2", "st_q3", "g0", "g1", "g2", "g3", "st_o0", "st_o1", "st_o2", "st_o3",
                 "line", "line2", "hid_k", "hid_v", "cmp_k", "st_kc", "cmp_v"]
        users += ["ga0", "ga1", "ga2", "ga3"]
        fill = [f"ga{n}" for n in range(4, KT)] + [f"gb{n}" for n in range(KT)]
        slots = [(qb, s) for qb in range(ST) for s in range(4)]
        fills = {}
        for n, name in enumerate(fill):
            fills[slots[4 + n]] = name
        for qb in range(1, ST):
            users += [fills[(qb, 0)], f"oT{qb - 1}"] + [fills[(qb, s)] for s in range(1, 4)]
        users.append(f"oT{ST - 1}")
        for n in range(KT):
            users += [f"ya{n}", f"yb{n}"]
        users += [f"wo{n}" for n in range(KT)] + ["st_x2"]
        USE = {name: n for n, name in enumerate(users)}
        U0 = len(users)

        def bank_of(name):
            return bank[USE[name] % 2]

        units = [(qb, h, b) for qb in range(ST) for h in range(NH) for b in range(2)]
        block = ctx.enter_context(nc.Block())

        @block.sync
        def _(sp):
            for n in range(2):
                sp.dma_start(x0[:, 4 * n:4 * n + 4, :], xT[:, 4 * n:4 * n + 4, :]).then_inc(x_in[n], 16)

            def load(c, slot):
                sp.dma_start(wraw[:, slot, :], w[c]).then_inc(w_landed[slot], 16)

            for c in range(FIRST):
                if c >= NRAW:
                    sp.wait_ge(w_split, c - NRAW + 1)
                load(c, c % NRAW)
            with sp.Fori(0, (N_CHUNKS - FIRST) // 4) as i:
                for j in range(4):
                    sp.wait_ge(w_split, 4 * i + (FIRST + j - NRAW + 1))
                    load(4 * i + (FIRST + j), (FIRST + j) % NRAW)

        @block.gpsimd
        def _(pool):
            def split(c, raw, two):
                pool.tensor_scalar(whi[:, two, :], wraw[:, raw, :], 1.0, 0.0, ALU.mult, ALU.add).then_inc(w_hi, 1)
                pool.wait_ge(w_hi, c + 1)
                pool.tensor_tensor(wlo[:, two, :], wraw[:, raw, :], whi[:, two, :].bitcast(F32),
                                   ALU.subtract).then_inc(w_split, 1)

            for c in range(FIRST):
                pool.wait_ge(w_landed[c % NRAW], 16 * (c // NRAW + 1))
                if c >= NSPLIT:
                    pool.wait_ge(w_used, c - NSPLIT + 1)
                split(c, c % NRAW, c % NSPLIT)
            with pool.Fori(0, (N_CHUNKS - FIRST) // 4) as i:
                for j in range(4):
                    c = FIRST + j
                    pool.wait_ge(w_landed[c % NRAW], 16 * i + 16 * (c // NRAW + 1))
                    pool.wait_ge(w_used, 4 * i + (c - NSPLIT + 1))
                    pool.sem_inc(w_open, 1)
                    split(4 * i + c, c % NRAW, c % NSPLIT)

        @block.tensor
        def _(pe):
            def take(name):
                c = AT[name]
                pe.wait_ge(w_split, c + 1)
                return whi[:, c % NSPLIT, :], wlo[:, c % NSPLIT, :]

            def claim(name):
                n = USE[name]
                if n >= 2:
                    pe.wait_ge(free[n % 2], n // 2)
                return bank[n % 2]

            def three(out_, wh, wl, mh, ml, first, last):
                pe.matmul(out_, wh, mh, start=first, stop=False)
                pe.matmul(out_, wh, ml, start=False, stop=False)
                return pe.matmul(out_, wl, mh, start=False, stop=last)

            def project(name, hi=None, lo=None, each_k=None):
                hi = hhi if hi is None else hi
                lo = hlo if lo is None else lo
                wh, wl = take(name)
                to = claim(name)
                for k in range(KT):
                    if each_k is not None:
                        each_k(k)
                    c = slice(k * P, k * P + P)
                    last = three(to[:], wh[:, c], wl[:, c], hi[:, k, :], lo[:, k, :], k == 0, k == KT - 1)
                last.then_inc(w_used, 1)

            stats = [0]

            def stat(name, matrix, squares, n=S):
                stats[0] += 1
                pe.wait_ge(stat_in, stats[0])
                to = claim(name)
                pe.matmul(to[:, 0:n], matrix, squares, start=True, stop=True).then_inc(stat_out, 1)

            pe.wait_ge(set_up, 3)
            stat("stat_x", ones[:], xsq[:, 0, :])

            def h_split(k):
                pe.wait_ge(h_lo, k + 1)

            for h in range(HG):
                project(f"f{h}", each_k=h_split if h == 0 else None)
                project(f"q{h}")

            def token_major(names, tiles, cols):
                k = 0
                for name, nk in zip(names, tiles):
                    wh, wl = take(name)
                    for kk in range(nk):
                        c = slice(kk * cols, kk * cols + cols)
                        for t in range(ST):
                            to = bank[2 + t][:, 0:cols]
                            hh, hl = hhi[:, k, t * P:t * P + P], hlo[:, k, t * P:t * P + P]
                            pe.matmul(to, hh, wh[:, c], start=k == 0, stop=False)
                            pe.matmul(to, hh, wl[:, c], start=False, stop=False)
                            last = pe.matmul(to, hl, wh[:, c], start=False, stop=k == KT - 1)
                        k += 1
                    last.then_inc(w_used, 1)
                    yield

            for _ in token_major([f"i{c}" for c in range(4)], [2] * 4, 512):
                pass

            sc_banks = [0]

            def sc_bank():
                n = sc_banks[0]
                if n >= 2:
                    pe.wait_ge(sc_kept[n % 2], n // 2)
                sc_banks[0] += 1
                return bank[6 + n % 2]

            def own(hs):
                for h in hs:
                    pe.wait_ge(kq_ready, h + 1)
                    to = sc_bank()
                    for t in range(ST):
                        c = slice(t * P, t * P + P)
                        last = pe.matmul(to[:, c], k_dec[:, h, c], q_raw[:, h, c], start=True, stop=True)
                    last.then_inc(sc_done, 1)

            def level(n):
                m = LEVELS[n]
                pe.wait_ge(decayed, n + 1)
                for pair in range(2):
                    to = sc_bank()
                    for h in (2 * pair, 2 * pair + 1):
                        for t in range(ST):
                            right = q_dec[:, h, t * P:t * P + P].rearrange("p (n two m) -> p n two m", two=2, m=m)
                            c = (h % 2) * 256 + t * 64
                            last = pe.matmul(to[:, c:c + 64].rearrange("p (n m) -> p n m", m=m),
                                             k_dec[:, h, t * P:t * P + P], right[:, :, 1, :], start=True, stop=True)
                    last.then_inc(sc_done, 1)

            def level_128():
                pe.wait_ge(decayed, 8)
                for pair in range(2):
                    to = sc_bank()
                    for h in (2 * pair, 2 * pair + 1):
                        for j in range(2):
                            c = (h % 2) * 256 + j * P
                            last = pe.matmul(to[:, c:c + P], k_dec[:, h, 2 * j * P:2 * j * P + P],
                                             q_dec[:, h, (2 * j + 1) * P:(2 * j + 2) * P], start=True, stop=True)
                    last.then_inc(sc_done, 1)

            def level_256(hs):
                pe.wait_ge(decayed, 9)
                for h in hs:
                    to = sc_bank()
                    for j in range(2):
                        last = pe.matmul(to[:, 256 * j:256 * j + 256], k_dec[:, h, j * P:j * P + P],
                                         q_dec[:, h, 256:512], start=True, stop=True)
                    last.then_inc(sc_done, 1)

            project("kc")
            own((0, 1))
            project("vc")
            own((2, 3))
            project("ks")
            level(0)
            project("kw")
            stat("st_ks", pair_ones[:], sq[:, 0, :])
            level(1)
            project("nq0")
            stat("st_kw", pair_ones[:], sq[:, 1, :])
            level(2)
            project("nq1")
            stat("st_q0", pair_ones[:], sq[:, 0, :])
            level(3)
            project("nq2")
            stat("st_q1", pair_ones[:], sq[:, 1, :])
            level(4)
            project("nq3")
            stat("st_q2", pair_ones[:], sq[:, 0, :])
            level(5)
            pe.wait_ge(tok_copied, 4)
            parts = token_major(["m0", "m1", "m2"], NM, MCOLS)
            next(parts)
            stat("st_q3", pair_ones[:], sq[:, 1, :])
            level(6)
            next(parts)
            level_128()
            next(parts)
            for _ in parts:
                pass
            level_256((0, 1))
            project("g0")
            level_256((2, 3))
            project("g1")

            pe.wait_ge(tok_copied, 8)
            for n in range(2):
                pe.wait_ge(sc_kept[n], 12)

            def mixed_values(h):
                to = bank[2 + h]
                for n, (s_t, t0, blk, nb) in enumerate(
                        [(0, 0, 0, 1), (0, 1, 4, 1), (0, 2, 6, 2), (1, 1, 1, 1), (1, 2, 8, 2), (2, 2, 2, 1),
                         (2, 3, 5, 1), (3, 3, 3, 1)]):
                    last = pe.matmul(to[:, t0 * P:(t0 + nb) * P], v_i[:, s_t, h * P:h * P + P],
                                     sc[:, h, blk:blk + nb, :].rearrange("p b t -> p (b t)"),
                                     start=n == 0, stop=n == 7, skip_group_check=True)
                last.then_inc(o_done, 1)

            for h in range(HG):
                mixed_values(h)
            project("g2")
            project("g3")
            for h in range(HG):
                stat(f"st_o{h}", ones[:], sq[:, h % 2, :])

            pe.wait_ge(consts_in, 16 * N_CONSTS)
            to = claim("line")
            pe.matmul(to[0:NH, 0:512], relx[:], ohs[:, 0:512], start=True, stop=True).then_inc(bias_line, 1)
            to = claim("line2")
            pe.matmul(to[0:NH, 0:128], relx[:], ohs[:, 512:TW], start=True, stop=True).then_inc(bias_line, 1)

            for j, name in enumerate(("hid_k", "hid_v")):
                to = claim(name)
                pe.wait_ge(xc_lo, j + 1)
                for half in range(2):
                    wh, wl = take(f"c{j}{half}")
                    for i in range(8):
                        n, c = 8 * half + i, slice(i * P, i * P + P)
                        last = three(to[:, 0:64], wh[:, c], wl[:, c], xhi[:, n].rearrange("p g c -> p (g c)"),
                                     xlo[:, n].rearrange("p g c -> p (g c)"), n == 0, n == 15)
                    last.then_inc(w_used, 1)
            pe.wait_ge(gel_ready, 1)
            to = claim("cmp_k")
            pe.matmul(to[:, 0:64], w2_k, gel[:, 0, :], start=True, stop=True).then_inc(cmp_out, 1)
            stat("st_kc", pair_ones[:], hid[:, 7, :], 64)
            pe.wait_ge(gel_ready, 2)
            to = claim("cmp_v")
            for g in range(2):
                for j in range(4):
                    last = pe.matmul(to[32 * j:32 * j + 32, g * 64:g * 64 + 64], gel[:, 1, g * 32:g * 32 + 32],
                                     w2_v, start=True, stop=True, skip_group_check=True)
            last.then_inc(cmp_out, 1)

            def q_tile(h, qb):
                g, i = divmod(h, 4)
                return qn[64 * g:64 * g + 64, i, qb * P:qb * P + P], slice(64 * g, 64 * g + 64)

            pe.wait_ge(normed, 6)
            pe.wait_ge(kcn_ready, 1)
            pe.wait_ge(o_free, 4)
            for qb in range(ST):
                if qb:
                    pe.wait_ge(cs_shift, qb)
                for h in range(NH):
                    q_, rows = q_tile(h, qb)
                    g, i = divmod(h, 4)
                    last = pe.matmul(bank[2 + g][:, 32 * i:32 * i + NCMP], q_, kcn[rows, 0:NCMP], start=True, stop=True)
                last.then_inc(cs_done, 1)
                project(f"ga{qb}")
                pe.wait_ge(cp_ready, qb + 1)
                for g in range(2):
                    last = pe.transpose(bank[4][:, g * P:g * P + P], pc[:, g * P:g * P + P], ident[:])
                last.then_inc(cpT_done, 1)
                pe.wait_ge(cpT_copied, qb + 1)
                pe.wait_ge(vbd_ready, 1)
                if qb:
                    pe.wait_ge(co_kept, qb)
                for g in range(2):
                    last = pe.matmul(bank[6][:, g * 256:g * 256 + 256], pcT[:, g, :], vbd[:, g, :],
                                     start=True, stop=True)
                last.then_inc(co_done, 1)
            pe.wait_ge(co_kept, ST)

            keys = (ksn, kwn)

            def scores(u):
                qb, h, b = units[u]
                if u >= 2:
                    pe.wait_ge(s_shift, u - 1)
                q_, rows = q_tile(h, qb)
                pe.matmul(bank[2 + u % 2][:, 0:(qb + 1) * P], q_, keys[b][rows, 0:(qb + 1) * P],
                          start=True, stop=True).then_inc(s_done, 1)

            def turn(u):
                qb, h, b = units[u]
                pe.wait_ge(p_ready, u + 1)
                if u >= 2:
                    pe.wait_ge(pt_ready[b], u // 2)
                for kb in range(qb + 1):
                    last = pe.transpose(bank[4 + b][:, kb * P:kb * P + P], p_ring[:, u % 4, kb * P:kb * P + P],
                                        ident[:])
                last.then_inc(t_done, 1)

            def values(u):
                qb, h, b = units[u]
                pe.wait_ge(pt_ready[b], u // 2 + 1)
                if qb and h == 0:
                    pe.wait_ge(ob_read, 2 * qb)
                g = h // 4
                for kb in range(qb + 1):
                    last = pe.matmul(bank[6 + b][:, h * 64:h * 64 + 64], pT[:, u % 3, kb * P:kb * P + P],
                                     v_sw[:, kb, b * P + g * 64:b * P + g * 64 + 64],
                                     start=kb == 0, stop=kb == qb)
                last.then_inc(pv_done, 1)

            def turn_out(qb):
                pe.wait_ge(ot_ready, qb + 1)
                to = claim(f"oT{qb}")
                for i in range(4):
                    last = pe.transpose(to[:, i * P:i * P + P], o_tok[:, qb, i * P:i * P + P], ident[:])
                last.then_inc(ot_done, 1)

            NU = len(units)
            for u in range(NU + 3):
                if u < NU:
                    scores(u)
                if 2 <= u < NU + 2:
                    turn(u - 2)
                if u >= 3:
                    values(u - 3)
                    qb, h, b = units[u - 3]
                    if (qb, h // 2) in fills and (h, b) == (h // 2 * 2 + 1, 1):
                        project(fills[(qb, h // 2)])
                    if qb and (h, b) == (1, 1):
                        turn_out(qb - 1)
            turn_out(ST - 1)

            pe.wait_ge(oa_lo, HG)
            pe.wait_ge(ob_lo, ST)
            for n in range(KT):
                wh, wl = take(f"ab{n}")
                for j, (hi, lo) in enumerate(((oahi, oalo), (obhi, oblo))):
                    to = claim(f"y{'ab'[j]}{n}")
                    for k in range(4):
                        c = slice((4 * j + k) * P, (4 * j + k + 1) * P)
                        last = three(to[:], wh[:, c], wl[:, c], hi[:, k, :], lo[:, k, :], k == 0, k == 3)
                last.then_inc(w_used, 1)

            def mix_split(k):
                pe.wait_ge(mix_lo, k + 1)

            for n in range(KT):
                project(f"wo{n}", each_k=mix_split if n == 0 else None)
            stat("st_x2", ones[:], tmp[:])

            for half in range(HALVES):
                c0 = N_STRAIGHT + half * 2 * UP_T
                r0 = U0 + half * (UP_T + KT)
                with pe.Fori(0, UP_T // 4) as i:
                    for j in range(4):
                        slot, b = (c0 + j) % NSPLIT, (r0 + j) % 2
                        pe.wait_ge(w_split, 4 * i + (c0 + j + 1))
                        pe.wait_ge(free[b], 2 * i + (r0 + j) // 2)
                        for k in range(KT):
                            if half == 0 and j == 0:
                                pe.wait_ge(h_lo, KT + k + 1)
                            c = slice(k * P, k * P + P)
                            last = three(bank[b][:], whi[:, slot, c], wlo[:, slot, c], hhi[:, k, :], hlo[:, k, :],
                                         k == 0, k == KT - 1)
                        last.then_inc(w_used, 1)
                c0 += UP_T
                r0 += UP_T
                with pe.Fori(0, KT // 2) as i:
                    for j in range(2):
                        b = (r0 + j) % 2
                        pe.wait_ge(free[b], i + (r0 + j) // 2)
                        for part in range(2):
                            slot = (c0 + 2 * j + part) % NSPLIT
                            pe.wait_ge(w_split, 4 * i + (c0 + 2 * j + part + 1))
                            for k in range(8):
                                kk = 8 * part + k
                                if j == 0:
                                    pe.wait_ge(u_lo, half * UP_T + kk + 1)
                                c = slice(k * P, k * P + P)
                                last = three(bank[b][:], whi[:, slot, c], wlo[:, slot, c], uhi[:, kk, :],
                                             ulo[:, kk, :], kk == 0, kk == 15)
                            last.then_inc(w_used, 1)

        @block.scalar
        def _(act):
            for dst, src in ((small[:, 0:SMALL], small_in), (mask_f[:], masks), (cst[:, 168:360], w2),
                             (ident[:], ident_in), (relx[0:32, :], rel), (ohs[:], oh)):
                act.dma_start(dst, src).then_inc(consts_in, 16)
            act.preload_act_table_set("natural_log_exp_and_others")

            steps = [0]

            def link(ins):
                steps[0] += 1
                ins.then_inc(act_step, 1)
                act.wait_ge(act_step, steps[0])

            rs = [0]
            outs = [0]

            def inverse_rms(name, dim, n=S):
                outs[0] += 1
                act.wait_ge(stat_out, outs[0])
                to = rstd[:, rs[0] % 2, 0:n]
                if rs[0] >= 2:
                    act.wait_ge(rs_used, rs[0] - 1)
                link(act.activation(to, bank_of(name)[:, 0:n], ACT.Ln, scale=1.0 / dim, bias=eps))
                act.activation(to, to, ACT.Exp, scale=-0.5).then_inc(rs_ready, 1)
                rs[0] += 1
                return to

            def leave(ins, name):
                ins.then_inc(free[USE[name] % 2], 1)

            for n in range(2):
                act.wait_ge(x_in[n], 16)
                act.activation(xsq[:, 4 * n:4 * n + 4, :], x0[:, 4 * n:4 * n + 4, :], ACT.Square).then_inc(x2_sq, 1)
            act.wait_ge(set_up, 3)
            inverse_rms("stat_x", D)
            for k in range(KT):
                act.wait_ge(hf_ready, k + 1)
                act.activation(hhi[:, k, :], hf[:, k % 2, :], ACT.Copy).then_inc(h_hi, 1)

            for h in range(HG):
                act.wait_ge(w_used, AT[f"f{h}"] + 1)
                if h == 0:
                    act.wait_ge(h_lo, KT)
                link(act.activation(e[:, h, :], bank_of(f"f{h}")[:], ACT.Exp, scale=-1.0))
                act.sem_inc(free[USE[f"f{h}"] % 2], 1)
                act.sem_inc(f_exp, 1)
                act.wait_ge(w_used, AT[f"q{h}"] + 1)
                link(act.activation(q_raw[:, h, :], bank_of(f"q{h}")[:], ACT.Copy))
                act.sem_inc(free[USE[f"q{h}"] % 2], 1)
                act.sem_inc(q_copied, 1)
            act.wait_ge(w_used, AT["i3"] + 1)
            for t in range(ST):
                act.activation(v_i[:, t, :], bank[2 + t][:], ACT.Copy).then_inc(tok_copied, 1)

            squares = [0]

            def raw_and_square(name, raw):
                act.wait_ge(w_used, AT[name] + 1)
                act.activation(raw, bank_of(name)[:], ACT.Copy).then_inc(raw_copied, 1)
                if squares[0] >= 2:
                    act.wait_ge(stat_out, squares[0])
                link(act.activation(sq[:, squares[0] % 2, :], bank_of(name)[:], ACT.Square))
                act.sem_inc(free[USE[name] % 2], 1)
                act.sem_inc(stat_in, 1)
                squares[0] += 1

            raw_and_square("ks", ksn[:])
            raw_and_square("kw", kwn[:])
            inverse_rms("st_ks", DH)
            raw_and_square("nq0", qn[:, 0, :])
            inverse_rms("st_kw", DH)
            raw_and_square("nq1", qn[:, 1, :])
            inverse_rms("st_q0", DH)
            raw_and_square("nq2", qn[:, 2, :])
            inverse_rms("st_q1", DH)
            raw_and_square("nq3", qn[:, 3, :])
            inverse_rms("st_q2", DH)
            inverse_rms("st_q3", DH)
            act.wait_ge(sc_done, 4 + 14 + 1)
            act.activation(sc[:, 0:2, 4:6, :].rearrange("p h b t -> p h (b t)"),
                           bank[6][:].rearrange("p (h t) -> p h t", h=2), ACT.Copy).then_inc(sc_kept[0], 1)
            act.wait_ge(sc_done, 4 + 14 + 2)
            act.activation(sc[:, 2:4, 4:6, :].rearrange("p h b t -> p h (b t)"),
                           bank[7][:].rearrange("p (h t) -> p h t", h=2), ACT.Copy).then_inc(sc_kept[1], 1)
            act.wait_ge(w_used, AT["m2"] + 1)
            for t in range(ST):
                act.activation(v_sw[:, t, :], bank[2 + t][:, 0:256], ACT.Copy)
                act.activation(gate3[:, t, :], bank[2 + t][:, 256:MCOLS], ACT.Exp, scale=-1.0).then_inc(tok_copied, 1)
            for h in range(HG):
                act.wait_ge(sc_done, 4 + 16 + h + 1)
                act.activation(sc[:, h, 6:10, :].rearrange("p b t -> p (b t)"), bank[6 + h % 2][:],
                               ACT.Copy).then_inc(sc_kept[h % 2], 1)
            for h in range(HG):
                act.wait_ge(w_used, AT[f"g{h}"] + 1)
                act.activation(gs[:, h, :], bank_of(f"g{h}")[:], ACT.Sigmoid).then_inc(g_sig, 1)
            for h in range(HG):
                act.wait_ge(o_done, h + 1)
                act.wait_ge(stat_out, 6 + h)
                act.activation(sq[:, h % 2, :], bank[2 + h][:], ACT.Square).then_inc(stat_in, 1)
                inverse_rms(f"st_o{h}", P)
                act.wait_ge(oa_f, h + 1)
                act.activation(oahi[:, h, :], tmp[:], ACT.Copy).then_inc(oa_hi, 1)

            act.wait_ge(bias_line, 2)
            link(act.activation(line[:], bank_of("line")[0:NH, 0:512], ACT.Copy, scale=-1.0))
            link(act.activation(line2[:], bank_of("line2")[0:NH, 0:128], ACT.Copy, scale=-1.0))
            act.sem_inc(free[USE["line"] % 2], 1)
            act.sem_inc(free[USE["line2"] % 2], 1)
            act.dma_start(scratch[:, 0:512], line[:]).then_inc(line_out, 16)
            act.dma_start(scratch[:, 512:TW], line2[:]).then_inc(line_out, 16)
            act.wait_ge(line_out, 32)
            act.dma_start(skewed, bass.AP(tensor=scratch.tensor, offset=P - 1, ap=[[TW, NH], [-1, P], [1, S]])
                          ).then_inc(skew_out, 16)
            act.wait_ge(skew_out, 16)
            for n in range(2):
                act.wait_ge(sc_kept[n], 12)
            act.wait_ge(decayed, 9)
            act.wait_ge(o_done, HG)
            act.dma_start(bias[:], skewed.rearrange("h p u -> p h u")).then_inc(bias_in, 16)

            for j in range(2):
                act.wait_ge(xc_f, j + 1)
                if j:
                    act.wait_ge(w_used, AT["c01"] + 1)
                act.activation(xhi[:], xf[:], ACT.Copy).then_inc(xc_hi, 1)
            for j in range(2):
                act.wait_ge(csum, j + 1)
                act.activation(hid[:, 3 * j + 2, :], hid[:, 3 * j + 1, :], ACT.Exp,
                               scale=-2.0 * 0.7978845608028654).then_inc(cexp, 1)
                if j == 0:
                    act.wait_ge(cmp_out, 1)
                    act.activation(hid[:, 7, :], bank_of("cmp_k")[:, 0:64], ACT.Square).then_inc(stat_in, 1)
            inverse_rms("st_kc", DH, 64)

            def copy_gate(name):
                act.wait_ge(w_used, AT[name] + 1)
                act.activation(gates[:, "ab".index(name[1]), int(name[2]), :], bank_of(name)[:], ACT.Copy
                               ).then_inc(free[USE[name] % 2], 1)

            for qb in range(ST):
                act.wait_ge(cs_shift, qb + 1)
                nc_ = 8 * qb + 7
                pcv = pc[:].rearrange("p (h c) -> p h c", h=NH)[:, :, 0:nc_]
                act.activation(pcv, pcv, ACT.Exp, scale=-1.0).then_inc(cp_ready, 1)
                copy_gate(f"ga{qb}")
                act.wait_ge(cpT_done, qb + 1)
                if qb:
                    act.wait_ge(co_done, qb)
                act.activation(pcT[:].rearrange("p g t -> p (g t)"), bank[4][:, 0:256], ACT.Copy).then_inc(cpT_copied, 1)

            def evacuate(u):
                qb, h, b = units[u]
                act.wait_ge(t_done, u + 1)
                if u >= 3:
                    act.wait_ge(pv_done, u - 2)
                act.activation(pT[:, u % 3, 0:(qb + 1) * P], bank[4 + b][:, 0:(qb + 1) * P], ACT.Copy
                               ).then_inc(pt_ready[b], 1)

            def out_high(qb):
                act.wait_ge(ot_done, qb + 1)
                act.activation(obhi[:, :, qb * P:qb * P + P], bank_of(f"oT{qb}")[:].rearrange("p (i t) -> p i t", i=4),
                               ACT.Copy).then_inc(ob_hi, 1)

            NU = len(units)
            for u in range(NU + 3):
                if u < NU:
                    qb, h, b = units[u]
                    n = (qb + 1) * P
                    act.wait_ge(s_shift, u + 1)
                    if qb >= 2 and h == 0 and b == 0:
                        act.wait_ge(ob_read, 2 * qb - 3)
                    act.activation(p_ring[:, u % 4, 0:n], p_ring[:, u % 4, 0:n], ACT.Exp, scale=-1.0,
                                   bias=mins[:, u % 4:u % 4 + 1], accum_out=sums[qb % 2][:, b, h:h + 1]).then_inc(p_ready, 1)
                if 2 <= u < NU + 2 and units[u - 2][2] == 0:
                    evacuate(u - 2)
                if u >= 3:
                    qb, h, b = units[u - 3]
                    if (qb, h // 2) in fills and (h, b) == (h // 2 * 2 + 1, 1):
                        copy_gate(fills[(qb, h // 2)])
                    if qb and (h, b) == (1, 1):
                        out_high(qb - 1)
            act.wait_ge(p_ready, NU)
            act.dma_start(x2[:], xT).then_inc(x_again, 16)
            out_high(ST - 1)

            for name in ("gb6", "gb7"):
                act.wait_ge(free[USE[name] % 2], USE[name] // 2 + 1)
            for n in range(4):
                act.activation(gates[:, n // 2, 4 * (n % 2):4 * (n % 2) + 4, :],
                               gates[:, n // 2, 4 * (n % 2):4 * (n % 2) + 4, :], ACT.Sigmoid).then_inc(gate_sig, 1)
            for n in range(KT):
                act.wait_ge(mix_f, n + 1)
                act.activation(hhi[:, n, :], rstd[:, n % 2, :], ACT.Copy).then_inc(mix_hi, 1)
            for n in range(KT):
                act.wait_ge(x2_ready, n + 1)
                if n >= 2:
                    act.wait_ge(sq_sum, n - 1)
                act.activation(sq[:, n % 2, :], x2[:, n, :], ACT.Square).then_inc(x2_sq, 1)
            rs[0] = 0
            outs[0] += 1
            act.wait_ge(stat_out, outs[0])
            link(act.activation(rstd[:, 0, :], bank_of("st_x2")[:], ACT.Ln, scale=1.0 / D, bias=eps))
            act.activation(rstd[:, 0, :], rstd[:, 0, :], ACT.Exp, scale=-0.5).then_inc(rs_ready, 1)
            for k in range(KT):
                act.wait_ge(hf_ready, KT + k + 1)
                act.activation(hhi[:, k, :], sq[:, k % 2, :], ACT.Copy).then_inc(h_hi, 1)

            for half in range(HALVES):
                c0 = N_STRAIGHT + half * 2 * UP_T
                r0 = U0 + half * (UP_T + KT)
                t0 = half * UP_T
                with act.Fori(0, UP_T // 4) as i:
                    for j in range(4):
                        b, s = (r0 + j) % 2, j % 2
                        act.wait_ge(w_used, 4 * i + (c0 + j + 1))
                        act.activation(r_ring[:, s, :], bank[b][:], ACT.Relu).then_inc(relu_d, 1)
                        act.wait_ge(u_f, 4 * i + (t0 + j + 1))
                        act.activation(uhi[:, 4 * i + j, :], u_ring[:, s, :], ACT.Copy).then_inc(u_hi, 1)
            for n in range(KT):
                act.wait_ge(y_ready, n + 1)
                act.dma_start(out[n], x2[:, n, :]).then_inc(y_out, 16)
            act.wait_ge(y_out, 16 * KT)

        @block.vector
        def _(dve):
            steps = [0]

            def link(ins):
                steps[0] += 1
                ins.then_inc(dve_step, 1)
                dve.wait_ge(dve_step, steps[0])

            def leave(ins, name):
                ins.then_inc(free[USE[name] % 2], 1)

            dve.memset(ones[:], 1.0).then_inc(set_up, 1)
            link(dve.memset(pair_ones[:], 0.0))
            dve.memset(pair_ones[0:64, 0:64], 1.0)
            dve.memset(eps, EPS)
            dve.memset(pair_ones[64:128, 64:128], 1.0).then_inc(set_up, 1)
            dve.memset(relx[32:33, :], -BIG).then_inc(set_up, 1)
            link(dve.memset(sc[:, :, 0:4, :], 0.0))

            dve.wait_ge(x2_sq, 2)
            link(dve.tensor_tensor(xsq[:, 0:4, :], xsq[:, 0:4, :], xsq[:, 4:8, :], ALU.add))
            link(dve.tensor_tensor(xsq[:, 0:2, :], xsq[:, 0:2, :], xsq[:, 2:4, :], ALU.add))
            dve.tensor_tensor(xsq[:, 0, :], xsq[:, 0, :], xsq[:, 1, :], ALU.add).then_inc(stat_in, 1)
            dve.wait_ge(consts_in, 16 * N_CONSTS)
            link(dve.tensor_scalar(g_q, g_q, -(DH ** -0.5), None, ALU.mult))
            dve.tensor_copy(mask[:, 0:7 * 256].rearrange("p (l t c) -> p l t c", l=7, t=4),
                            mask_f[:, 0:7 * 64].rearrange("p (l one c) -> p l one c", l=7, one=1)
                            .broadcast_to([P, 7, 4, 64]))
            link(dve.tensor_copy(mask[:, 7 * 256:].rearrange("p (t c) -> p t c", t=4),
                                 mask_f[:, 7 * 64:].rearrange("p (one c) -> p one c", one=1)
                                 .broadcast_to([P, 4, P])))

            def norm_to_h(x_, gain, rs_, ring, n0):
                for k in range(KT):
                    if k >= 2:
                        dve.wait_ge(h_lo, n0 + k - 1)
                    dve.scalar_tensor_tensor(ring[:, k % 2, :], x_[:, k, :], gain[:, k:k + 1], rs_, ALU.mult,
                                             ALU.mult).then_inc(hf_ready, 1)
                    if k >= 1:
                        low(k - 1, ring, n0)
                low(KT - 1, ring, n0)

            def low(k, ring, n0):
                dve.wait_ge(h_hi, n0 + k + 1)
                dve.tensor_tensor(hlo[:, k, :], ring[:, k % 2, :], hhi[:, k, :].bitcast(F32),
                                  ALU.subtract).then_inc(h_lo, 1)

            dve.wait_ge(rs_ready, 1)
            dve.sem_inc(free[USE["stat_x"] % 2], 1)
            norm_to_h(x0, g_mix, rstd[:, 0, :], hf, 0)
            dve.wait_ge(h_lo, KT)
            dve.sem_inc(rs_used, 1)

            for h in range(HG):
                dve.wait_ge(f_exp, h + 1)
                link(dve.tensor_scalar(f[:, h, :], e[:, h, :], BIG, 1.0, ALU.min, ALU.add))
                link(dve.reciprocal(f[:, h, :], f[:, h, :]))
                link(dve.scalar_tensor_tensor(k_dec[:, h, :], e[:, h, :], BIG, f[:, h, :], ALU.min, ALU.mult))
                dve.wait_ge(q_copied, h + 1)
                dve.tensor_tensor(q_dec[:, h, :], q_raw[:, h, :], f[:, h, :], ALU.mult).then_inc(kq_ready, 1)
            dve.wait_ge(kq_ready, HG)
            dve.sem_inc(decayed, 1)

            def copy_raw(name, to):
                dve.wait_ge(w_used, AT[name] + 1)
                link(dve.tensor_copy(to, bank_of(name)[:]))
                dve.sem_inc(free[USE[name] % 2], 1)

            def keep_own(hs):
                for h in hs:
                    dve.wait_ge(sc_done, h + 1)
                    dve.copy_predicated(sc[:, h, 0:4, :].rearrange("p b t -> p (b t)"), mask[:, 7 * 256:],
                                        bank[6 + h % 2][:]).then_inc(sc_kept[h % 2], 1)

            tot_at = {}
            o_ = 0
            for m in LEVELS[1:]:
                tot_at[m] = (o_, HG * S // m)
                o_ += HG * S // m

            def totals(m):
                if m == 1:
                    return f[:].rearrange("p h t -> p (h t)")
                return tot[:, tot_at[m][0]:tot_at[m][0] + tot_at[m][1]]

            def advance(n):
                m = LEVELS[n]
                nb = HG * S // (2 * m)
                t = totals(m).rearrange("p (n two) -> p n two", two=2)
                kv = k_dec[:].rearrange("p h t -> p (h t)").rearrange("p (n two m) -> p n two m", two=2, m=m)
                qv = q_dec[:].rearrange("p h t -> p (h t)").rearrange("p (n two m) -> p n two m", two=2, m=m)
                dve.tensor_tensor(totals(2 * m).rearrange("p (n one) -> p n one", one=1), t[:, :, 0:1], t[:, :, 1:2],
                                  ALU.mult)
                dve.tensor_tensor(kv[:, :, 0, :], kv[:, :, 0, :], t[:, :, 1:2].broadcast_to([P, nb, m]), ALU.mult)
                link(dve.tensor_tensor(qv[:, :, 1, :], qv[:, :, 1, :], t[:, :, 0:1].broadcast_to([P, nb, m]),
                                       ALU.mult))
                dve.sem_inc(decayed, 1)

            def keep_level(n):
                m = LEVELS[n]
                for h in range(HG):
                    c = (h % 2) * 256
                    to = sc[:, h, 0:4, :].rearrange("p b t -> p (b t)").rearrange("p (n two m) -> p n two m",
                                                                                 two=2, m=m)
                    ins = dve.copy_predicated(to[:, :, 1, :],
                                              mask[:, n * 256:n * 256 + 256].rearrange("p (n m) -> p n m", m=m),
                                              bank[6 + h // 2][:, c:c + 256].rearrange("p (n m) -> p n m", m=m))
                    if h % 2:
                        ins.then_inc(sc_kept[h // 2], 1)

            normed_n = [0]

            def norm(raw, gain):
                n = normed_n[0]
                dve.wait_ge(rs_ready, n + 2)
                dve.wait_ge(raw_copied, n + 1)
                link(dve.scalar_tensor_tensor(raw, raw, gain, rstd[:, (n + 1) % 2, :], ALU.mult, ALU.mult))
                dve.sem_inc(rs_used, 1)
                dve.sem_inc(normed, 1)
                normed_n[0] += 1

            def leave_stat(name):
                dve.sem_inc(free[USE[name] % 2], 1)

            copy_raw("kc", kc_raw[:])
            keep_own((0, 1))
            copy_raw("vc", vc_raw[:])
            keep_own((2, 3))
            for n in range(7):
                dve.wait_ge(sc_done, 4 + 2 * n + 2)
                advance(n)
                keep_level(n)
                if n >= 1:
                    name, raw, gain = (("st_ks", ksn[:], g_ks), ("st_kw", kwn[:], g_kw), ("st_q0", qn[:, 0, :], g_q),
                                       ("st_q1", qn[:, 1, :], g_q), ("st_q2", qn[:, 2, :], g_q),
                                       ("st_q3", qn[:, 3, :], g_q))[n - 1]
                    norm(raw, gain)
                    leave_stat(name)
            dve.wait_ge(sc_done, 4 + 14 + 2)
            advance(7)
            dve.wait_ge(tok_copied, 8)
            link(dve.tensor_scalar(gate3, gate3, 1.0, None, ALU.add))
            link(dve.reciprocal(gate3, gate3))
            for h in range(HG):
                dve.wait_ge(g_sig, h + 1)
                link(dve.scalar_tensor_tensor(gs[:, h, :], bank_of(f"g{h}")[:], g_hg, gs[:, h, :], ALU.mult, ALU.mult))
                leave_stat(f"g{h}")
            for h in range(HG):
                dve.wait_ge(rs_ready, 8 + h)
                leave_stat(f"st_o{h}")
                if h:
                    dve.wait_ge(oa_lo, h)
                link(dve.tensor_tensor(tmp[:], bank[2 + h][:], rstd[:, (7 + h) % 2, :], ALU.mult))
                dve.sem_inc(rs_used, 1)
                dve.sem_inc(o_free, 1)
                link(dve.tensor_tensor(tmp[:], tmp[:], gs[:, h, :], ALU.mult))
                dve.sem_inc(oa_f, 1)
                dve.wait_ge(oa_hi, h + 1)
                dve.tensor_tensor(oalo[:, h, :], tmp[:], oahi[:, h, :].bitcast(F32), ALU.subtract).then_inc(oa_lo, 1)

            for n in range(2):
                dve.wait_ge(sc_kept[n], 12)
            dve.wait_ge(o_done, HG)
            link(dve.memset(xf[:], 0.0))
            for j, (raw, pos_) in enumerate(((kc_raw, pos_k), (vc_raw, pos_v))):
                if j:
                    dve.wait_ge(xc_hi, 1)
                    dve.wait_ge(xc_lo, 1)
                for par in range(2):
                    for g in range(2):
                        v = raw[64 * g:64 * g + 64, :].rearrange("p (n b two) -> p b n two", b=8, two=2)
                        for a in range(2):
                            last = dve.tensor_copy(xf[64 * par:64 * par + 64, 8 * a:8 * a + 8, g, 0:NCMP],
                                                   v[:, :, a:a + NCMP, par])
                link(last)
                for g in range(2):
                    last = dve.tensor_tensor(xf[:, :, g, 0:NCMP], xf[:, :, g, 0:NCMP],
                                             pos_.rearrange("p (n one) -> p n one", one=1).broadcast_to([P, 16, NCMP]),
                                             ALU.add)
                link(last)
                dve.sem_inc(xc_f, 1)
                dve.wait_ge(xc_hi, j + 1)
                if j:
                    dve.wait_ge(w_used, AT["c01"] + 1)
                dve.tensor_tensor(xlo[:], xf[:], xhi[:].bitcast(F32), ALU.subtract).then_inc(xc_lo, 1)

            for j in range(2):
                u_, t_, e_ = (hid[:, 3 * j + n, :] for n in range(3))
                dve.wait_ge(w_used, AT[f"c{j}1"] + 1)
                name = ("hid_k", "hid_v")[j]
                link(dve.tensor_scalar(u_, bank_of(name)[:, 0:64], (b1_k, b1_v)[j], None, ALU.add))
                leave_stat(name)
                link(dve.tensor_tensor(t_, u_, u_, ALU.mult))
                link(dve.tensor_scalar(t_, t_, 0.044715, 1.0, ALU.mult, ALU.add))
                link(dve.tensor_tensor(t_, t_, u_, ALU.mult))
                link(dve.tensor_scalar(t_, t_, -50.0, None, ALU.max))
                dve.sem_inc(csum, 1)
                dve.wait_ge(cexp, j + 1)
                link(dve.tensor_scalar(e_, e_, 1.0, None, ALU.add))
                link(dve.reciprocal(e_, e_))
                dve.tensor_tensor(gel[:, j, :], u_, e_, ALU.mult).then_inc(gel_ready, 1)
            dve.wait_ge(rs_ready, 12)
            leave_stat("st_kc")
            rs_ = rstd[:, 11 % 2, 0:64]
            for g in range(2):
                rows = slice(64 * g, 64 * g + 64)
                last = dve.scalar_tensor_tensor(kcn[rows, :], bank_of("cmp_k")[rows, 32 * g:32 * g + 32], g_kc[rows, :],
                                                rs_[rows, 32 * g:32 * g + 32], ALU.mult, ALU.mult)
            link(last)
            dve.sem_inc(kcn_ready, 1)
            leave_stat("cmp_k")
            link(dve.memset(vbd[:], 0.0))
            dve.memset(pc[:], 0.0)
            dve.wait_ge(cmp_out, 2)
            for g in range(2):
                for j in range(4):
                    last = dve.tensor_copy(vbd[32 * j:32 * j + 32, g, 64 * j:64 * j + 64],
                                           bank_of("cmp_v")[32 * j:32 * j + 32, 64 * g:64 * g + 64])
            link(last)
            dve.sem_inc(vbd_ready, 1)
            leave_stat("cmp_v")

            def by_head(v):
                return v.rearrange("p (h one) -> p h one", one=1)

            for qb in range(ST):
                nc_ = 8 * qb + 7
                dve.wait_ge(cs_done, qb + 1)
                if qb == 0:
                    dve.wait_ge(bias_in, 16)
                else:
                    dve.wait_ge(cpT_done, qb)
                pcv = pc[:].rearrange("p (h c) -> p h c", h=NH)[:, :, 0:nc_]
                s0 = 415 - 128 * qb
                for g in range(2):
                    hs = slice(4 * g, 4 * g + 4)
                    last = dve.tensor_tensor(
                        pcv[:, hs, :], bank[2 + g][:, 0:P].rearrange("p (h c) -> p h c", h=4)[:, :, 0:nc_],
                        bias[:, hs, s0:s0 + 16 * (nc_ - 1) + 1:16], ALU.add)
                link(last)
                link(dve.tensor_reduce(mc, pcv, AX_X, ALU.min))
                link(dve.tensor_tensor(pcv, pcv, by_head(mc).broadcast_to([P, NH, nc_]), ALU.subtract))
                dve.sem_inc(cs_shift, 1)
                dve.tensor_scalar(okc, mc, BIG / 10, None, ALU.is_lt)
                dve.wait_ge(cp_ready, qb + 1)
                link(dve.tensor_reduce(sumc, pcv, AX_X, ALU.add))
                link(dve.reciprocal(wc, sumc))
                link(dve.tensor_tensor(wc, wc, okc, ALU.mult))
                g3 = gate3[:, qb, :].rearrange("p (h c) -> p h c", c=3)
                link(dve.tensor_tensor(by_head(wc), by_head(wc), g3[:, :, 0:1], ALU.mult))
                dve.wait_ge(co_done, qb + 1)
                dve.tensor_tensor(o_tok[:, qb, :].rearrange("p (h d) -> p h d", h=NH),
                                  bank[6][:].rearrange("p (h d) -> p h d", h=NH),
                                  by_head(wc).broadcast_to([P, NH, DH]), ALU.mult).then_inc(co_kept, 1)

            def evacuate(u):
                qb, h, b = units[u]
                dve.wait_ge(t_done, u + 1)
                if u >= 3:
                    dve.wait_ge(pv_done, u - 2)
                dve.tensor_copy(pT[:, u % 3, 0:(qb + 1) * P], bank[4 + b][:, 0:(qb + 1) * P]).then_inc(pt_ready[b], 1)

            def weigh(qb):
                dve.wait_ge(p_ready, 16 * qb + 16)
                link(dve.reciprocal(wts, sums[qb % 2]))
                dve.sem_inc(ob_read, 1)
                g3 = gate3[:, qb, :].rearrange("p (h c) -> p c h", c=3)
                link(dve.tensor_tensor(wts, wts, g3[:, 1:3, :], ALU.mult))
                dve.wait_ge(pv_done, 16 * qb + 16)
                acc = o_tok[:, qb, :]
                for b in range(2):
                    link(dve.tensor_tensor(tmp[:].rearrange("p (h d) -> p h d", h=NH),
                                           bank[6 + b][:].rearrange("p (h d) -> p h d", h=NH),
                                           by_head(wts[:, b, :]).broadcast_to([P, NH, DH]), ALU.mult))
                    if b == 1:
                        dve.sem_inc(ob_read, 1)
                    link(dve.tensor_tensor(acc, acc, tmp[:], ALU.add))
                dve.sem_inc(ot_ready, 1)

            def out_low(qb):
                dve.wait_ge(ob_hi, qb + 1)
                c = slice(qb * P, qb * P + P)
                link(dve.tensor_tensor(oblo[:, :, c], bank_of(f"oT{qb}")[:].rearrange("p (i t) -> p i t", i=4),
                                       obhi[:, :, c].bitcast(F32), ALU.subtract))
                dve.sem_inc(ob_lo, 1)
                leave_stat(f"oT{qb}")

            NU = len(units)
            for u in range(NU + 3):
                if u < NU:
                    qb, h, b = units[u]
                    n = (qb + 1) * P
                    dve.wait_ge(s_done, u + 1)
                    if u >= 4:
                        dve.wait_ge(t_done, u - 3)
                    dve.tensor_tensor_reduce(out=p_ring[:, u % 4, 0:n], in0=bank[2 + u % 2][:, 0:n],
                                             in1=bias[:, h, S - n:S], scale=1.0, scalar=3.0e38, op0=ALU.add,
                                             op1=ALU.min, accum_out=mins[:, u % 4:u % 4 + 1]).then_inc(s_shift, 1)
                if 2 <= u < NU + 2 and units[u - 2][2] == 1:
                    evacuate(u - 2)
                if u >= 3:
                    qb, h, b = units[u - 3]
                    if (h, b) == (NH - 1, 1):
                        weigh(qb)
                    if qb and (h, b) == (1, 1):
                        out_low(qb - 1)
            out_low(ST - 1)

            dve.wait_ge(gate_sig, 4)
            def mix_low(n):
                dve.wait_ge(mix_hi, n + 1)
                dve.tensor_tensor(hlo[:, n, :], rstd[:, n % 2, :], hhi[:, n, :].bitcast(F32),
                                  ALU.subtract).then_inc(mix_lo, 1)

            for n in range(KT):
                dve.wait_ge(w_used, AT[f"ab{n}"] + 1)
                if n >= 2:
                    dve.wait_ge(mix_lo, n - 1)
                for j, name in enumerate((f"ya{n}", f"yb{n}")):
                    last = dve.tensor_tensor(gates[:, j, n, :], gates[:, j, n, :], bank_of(name)[:], ALU.mult)
                link(last)
                leave_stat(f"ya{n}")
                leave_stat(f"yb{n}")
                dve.tensor_tensor(rstd[:, n % 2, :], gates[:, 0, n, :], gates[:, 1, n, :], ALU.add).then_inc(mix_f, 1)
                if n:
                    mix_low(n - 1)
            mix_low(KT - 1)
            dve.wait_ge(x_again, 16)
            for n in range(KT):
                dve.wait_ge(w_used, AT[f"wo{n}"] + 1)
                link(dve.tensor_tensor(x2[:, n, :], x2[:, n, :], bank_of(f"wo{n}")[:], ALU.add))
                dve.sem_inc(x2_ready, 1)
                leave_stat(f"wo{n}")
                dve.wait_ge(x2_sq, 2 + n + 1)
                if n == 0:
                    link(dve.tensor_copy(tmp[:], sq[:, 0, :]))
                else:
                    link(dve.tensor_tensor(tmp[:], tmp[:], sq[:, n % 2, :], ALU.add))
                dve.sem_inc(sq_sum, 1)
            dve.sem_inc(stat_in, 1)
            dve.wait_ge(rs_ready, 13)
            leave_stat("st_x2")
            norm_to_h(x2, g_mlp, rstd[:, 0, :], sq, KT)

            for half in range(HALVES):
                c0 = N_STRAIGHT + half * 2 * UP_T
                r0 = U0 + half * (UP_T + KT)
                t0 = half * UP_T
                with dve.Fori(0, UP_T // 4) as i:
                    for j in range(4):
                        b, s = (r0 + j) % 2, j % 2
                        dve.wait_ge(relu_d, 4 * i + (t0 + j + 1))
                        dve.tensor_tensor(u_ring[:, s, :], bank[b][:], r_ring[:, s, :], ALU.mult).then_inc(u_f, 1)
                        dve.wait_ge(u_hi, 4 * i + (t0 + j + 1))
                        dve.sem_inc(free[b], 1)
                        dve.tensor_tensor(ulo[:, 4 * i + j, :], u_ring[:, s, :], uhi[:, 4 * i + j, :].bitcast(F32),
                                          ALU.subtract).then_inc(u_lo, 1)
                c0 += UP_T
                r0 += UP_T
                with dve.Fori(0, KT // 2) as i:
                    for j in range(2):
                        b = (r0 + j) % 2
                        dve.wait_ge(w_used, 4 * i + (c0 + 2 * j + 2))
                        if half == 0:
                            dve.tensor_tensor(x2[:, 2 * i + j, :], x2[:, 2 * i + j, :], bank[b][:], ALU.add
                                              ).then_inc(free[b], 1)
                        else:
                            dve.tensor_tensor(x2[:, 2 * i + j, :], x2[:, 2 * i + j, :], bank[b][:], ALU.add
                                              ).then_inc(y_ready, 1)
                            dve.wait_ge(y_ready, 2 * i + (j + 1))
                            dve.sem_inc(free[b], 1)


def make_oh():
    dist = 511 - np.arange(TW)
    d = np.maximum(dist, 0)
    df = np.maximum(d, 1).astype(np.float32)
    large = 16 + (np.log(df / np.float32(16)) / np.float32(np.log(64.0)) * np.float32(16)).astype(np.int32)
    bucket = np.where(d < 16, d, np.minimum(large, 31))
    oh = np.zeros((33, TW), np.float32)
    oh[np.where(dist >= 0, bucket, 32), np.arange(TW)] = 1.0
    return oh


def make_masks():
    s = np.arange(P)[:, None]
    parts = []
    for m in LEVELS[:7]:
        n = np.arange(64)[None, :] // m
        parts.append((s // (2 * m) == n) & (s % (2 * m) < m))
    parts.append(np.eye(P, dtype=bool))
    return np.concatenate(parts, 1).astype(np.float32)


def lay_out(inputs):
    sizes = [512, 512, 512, 512, 512] + [128] * 6 + [24, 1024, 1024]
    offs = np.cumsum([0] + sizes)
    w_in = inputs["w_in"][0]
    hq, hf_, hi, hg, nq, kc, vc, ks, vs, kw, vw, ng, ga, gb = (
        w_in[:, offs[n]:offs[n + 1]] for n in range(14))

    def tiles(m):
        return m.reshape(-1, P, m.shape[1]).transpose(1, 0, 2).reshape(P, -1)

    w = np.zeros((N_CHUNKS, P, CW), np.float32)
    for h in range(4):
        c = slice(h * P, h * P + P)
        w[AT[f"f{h}"]] = tiles(hf_[:, c])
        w[AT[f"q{h}"]] = tiles(hq[:, c])
        w[AT[f"g{h}"]] = tiles(hg[:, c])
        w[AT[f"i{h}"]] = tiles(hi[256 * h:256 * h + 256])
        w[AT[f"nq{h}"]] = tiles(np.concatenate([nq[:, 64 * h:64 * h + 64], nq[:, 256 + 64 * h:320 + 64 * h]], 1))
    for name, m in (("kc", kc), ("vc", vc), ("ks", ks), ("kw", kw)):
        w[AT[name]] = tiles(m)
    m = np.concatenate([vs, vw, ng], 1)
    k = 0
    for n, nk in enumerate(NM):
        w[AT[f"m{n}"], :, 0:nk * MCOLS] = tiles(m[k * P:(k + nk) * P])
        k += nk
    w1 = inputs["cmp_w1"][0]
    for j in range(2):
        for half in range(2):
            w[AT[f"c{j}{half}"]] = tiles(w1[j, 1024 * half:1024 * half + 1024])
    wa, wb, wo = inputs["w_branch_a"][0], inputs["w_branch_b"][0], inputs["w_out"][0]
    for n in range(KT):
        c = slice(n * P, n * P + P)
        w[AT[f"ga{n}"]] = tiles(ga[:, c])
        w[AT[f"gb{n}"]] = tiles(gb[:, c])
        w[AT[f"ab{n}"], :, 0:512] = tiles(wa[:, c])
        w[AT[f"ab{n}"], :, 512:1024] = tiles(wb[:, c])
        w[AT[f"wo{n}"]] = tiles(wo[:, c])
    up, down = inputs["w_up"][0], inputs["w_down"][0]
    at = N_STRAIGHT
    for half in range(HALVES):
        for n in range(UP_T):
            c = (half * UP_T + n) * P
            w[at] = tiles(up[:, c:c + P])
            at += 1
        for n in range(KT):
            for part in range(2):
                r = (half * UP_T + 8 * part) * P
                w[at] = tiles(down[r:r + 1024, n * P:n * P + P])
                at += 1
    gqk = inputs["nsa_qk_gain"][0]
    pos = inputs["cmp_pos"][0].reshape(2, 16, 2, 64).transpose(2, 3, 0, 1).reshape(P, 32)
    w2 = inputs["cmp_w2"][0]
    return {
        "xT": inputs["x"][0].T.reshape(KT, P, S).transpose(1, 0, 2),
        "w": w,
        "oh": make_oh(),
        "masks": make_masks(),
        "ident_in": np.eye(P, dtype=np.float32),
        "small_in": np.concatenate([
            inputs["norm_mix"][0].reshape(KT, P).T, inputs["norm_mlp"][0].reshape(KT, P).T,
            inputs["hg_out_gain"][0].reshape(P, 1), np.concatenate([gqk.T, gqk.T], 0),
            inputs["cmp_b1"][0].T, pos], 1),
        "w2": np.concatenate([w2[0], w2[0], w2[1]], 1),
        "rel": inputs["rel_bias"],
    }


def kernel(**inputs):
    import concourse.bacc as bacc
    from concourse.bass_utils import run_bass_kernel_spmd

    nc = bacc.Bacc("TRN2", target_bir_lowering=False, num_devices=1)
    arrays = {f"in_{n}": np.ascontiguousarray(a) for n, a in lay_out(
        {n: np.asarray(a) for n, a in inputs.items()}).items()}
    aps = {n[3:]: nc.dram_tensor(n, a.shape, mybir.dt.from_np(a.dtype), kind="ExternalInput").ap()
           for n, a in arrays.items()}
    scratch = nc.dram_tensor("bias_lines", (NH, TW), F32, kind="Internal").ap()
    skewed = nc.dram_tensor("bias_skewed", (NH, P, S), F32, kind="Internal").ap()
    out = nc.dram_tensor("out", (KT, P, S), F32, kind="ExternalOutput").ap()
    build_block(nc, scratch=scratch, skewed=skewed, out=out, **aps)
    r = run_bass_kernel_spmd(nc, [arrays], core_ids=[0])
    return r.results[0]["out"].reshape(1, D, S).transpose(0, 2, 1)
```

```python
from contextlib import ExitStack

import numpy as np

import concourse.bass as bass
from concourse import mybir

F32 = mybir.dt.float32
F32R = mybir.dt.float32r
U8 = mybir.dt.uint8
ACT = mybir.ActivationFunctionType
ALU = mybir.AluOpType
AX_X = mybir.AxisListType.X

P = 128
D = 1024
S = 512
KT = D // P
ST = S // P
HG = 4
NH = 8
DH = 64
NCMP = 31
FF = 4096
EPS = 1e-6
BIG = 1e30
CW = 1024
NRAW = 4
NSPLIT = 2
LEVELS = [1, 2, 4, 8, 16, 32, 64, 128, 256]
TW = 640

CHUNKS = [f"{a}{h}" for h in range(HG) for a in "fq"] + [f"i{c}" for c in range(4)]
CHUNKS += ["kc", "vc", "ks", "kw", "nq0", "nq1", "nq2", "nq3", "m0", "m1", "m2"]
CHUNKS += ["c00", "g0", "c01", "g1", "c10", "g2", "c11", "g3"]
CHUNKS += [f"{a}{n}" for a in ("ga", "gb") for n in range(KT)]
CHUNKS += [f"ab{n}" for n in range(KT)] + [f"wo{n}" for n in range(KT)]
N_STRAIGHT = len(CHUNKS)
HALVES = 2
UP_T = FF // P // HALVES
N_CHUNKS = N_STRAIGHT + HALVES * (UP_T + KT * UP_T // KT)
AT = {name: n for n, name in enumerate(CHUNKS)}
FIRST = N_CHUNKS % 4 + 4

SMALL = 55
N_CONSTS = 6
LAG_T, LAG_V = 3, 4
MCOLS = 280
NM = [3, 3, 2]


def build_block(nc, xT, w, oh, masks, ident_in, small_in, w2, rel, scratch, skewed, out):
    with ExitStack() as ctx:
        base = (nc.sbuf_base + 31) // 32 * 32

        def at(name, kb, shape, dt=F32):
            return nc.alloc_sbuf_tensor_at(name, shape, dt, offset=base + int(kb * 1024))

        def sem(name):
            return ctx.enter_context(nc.semaphore(name))

        ones = at("ones", 0, [P, P])
        pair_ones = at("pair_ones", 0.5, [P, P])
        ident = at("ident", 1, [P, P])
        mask = at("mask", 1.5, [P, 7 * 256 + 512], U8)
        mask_f = at("mask_f", 190.5, [P, 7 * 64 + P])
        small = at("small", 3.75, [P, 128])
        g_mix, g_mlp = small[:, 0:8], small[:, 8:16]
        g_hg, g_q, g_kc, g_ks, g_kw, b1_k, b1_v = (small[:, n:n + 1] for n in range(16, 23))
        pos_k, pos_v = small[:, 23:39], small[:, 39:55]
        eps = small[:, 64:65]
        hhi = at("hhi", 4.5, [P, KT, S], F32R)
        hlo = at("hlo", 20.5, [P, KT, S], F32R)
        wraw = at("wraw", 36.5, [P, NRAW, CW])
        whi = at("whi", 52.5, [P, NSPLIT, CW], F32R)
        wlo = at("wlo", 60.5, [P, NSPLIT, CW], F32R)
        x0 = at("x0", 68.5, [P, KT, S])
        xsq = at("xsq", 84.5, [P, KT, S])
        hf = at("hf", 100.5, [P, 2, S])
        q_raw = at("q_raw", 68.5, [P, HG, S])
        q_dec = at("q_dec", 76.5, [P, HG, S])
        k_dec = at("k_dec", 84.5, [P, HG, S])
        f = at("f", 92.5, [P, HG, S])
        e = at("e", 100.5, [P, HG, S])
        tot = at("tot", 100.5, [P, HG * S])
        sc = at("sc", 108.5, [P, HG, 10, P])
        v_i = at("v_i", 128.5, [P, ST, S])
        gs = at("gs", 136.5, [P, HG, S])
        oahi = at("oahi", 144.5, [P, HG, S], F32R)
        oalo = at("oalo", 152.5, [P, HG, S], F32R)
        qn = at("qn", 160.5, [P, 4, S])
        ksn = at("ksn", 168.5, [P, S])
        kwn = at("kwn", 170.5, [P, S])
        v_sw = at("v_sw", 172.5, [P, ST, 256])
        kc_raw = at("kc_raw", 176.5, [P, S])
        vc_raw = at("vc_raw", 178.5, [P, S])
        sq = at("sq", 180.5, [P, 2, S])
        rstd = at("rstd", 184.5, [P, 2, S])
        tmp = at("tmp", 188.5, [P, S])
        oblo = at("oblo", 190.5, [P, 4, S], F32R)
        pT = at("pT", 198.5, [P, 3, S])
        cst = at("cst", 204.5, [P, 384])
        gates = at("gates", 68.5, [P, 2, KT, S])
        bias = at("bias", 100.5, [P, NH, S])
        xf = [at("xf_k", 190.5, [P, 16, 2, 32]), at("xf_v", 144.5, [P, 16, 2, 32])]
        xhi = [at("xhi_k", 194.5, [P, 16, 2, 32], F32R), at("xhi_v", 148.5, [P, 16, 2, 32], F32R)]
        xlo = [at("xlo_k", 198.5, [P, 16, 2, 32], F32R), at("xlo_v", 152.5, [P, 16, 2, 32], F32R)]
        o_ring = at("o_ring", 190.5, [P, 2, S])
        p_ring = at("p_ring", 128.5, [P, 4, S])
        obhi = at("obhi", 136.5, [P, 4, S], F32R)
        o_tok = at("o_tok", 116.5, [P, ST, S])
        vbd = at("vbd", 176.5, [P, 2, 256])
        pc = at("pc", 126.5, [P, 256])
        pcT = at("pcT", 127.5, [P, 2, P])
        x2 = at("x2", 100.5, [P, KT, S])
        uhi = at("uhi", 116.5, [P, UP_T, S], F32R)
        ulo = at("ulo", 148.5, [P, UP_T, S], F32R)
        ghi = at("ghi", 68.5, [P, KT, S], F32R)
        glo = at("glo", 84.5, [P, KT, S], F32R)
        r_ring = at("r_ring", 4.5, [P, 2, S])
        u_ring = at("u_ring", 8.5, [P, 2, S])
        t_ring = at("t_ring", 12.5, [P, 2, S])
        gate3 = cst[:, 0:96].rearrange("p (t c) -> p t c", t=ST)
        sums = [cst[:, n:n + 16].rearrange("p (b h) -> p b h", b=2) for n in (96, 360)]
        wts = cst[:, 112:128].rearrange("p (b h) -> p b h", b=2)
        mins = small[:, 80:96].rearrange("p (r h) -> p r h", r=4)
        mc, sumc, okc = (cst[:, n:n + 8] for n in (136, 144, 160))
        wcs = [cst[:, 152:160], small[:, 96:104]]
        w2_k, w2_v = cst[:, 168:296], cst[:, 296:360]
        relx = at("relx", 198.5, [33, NH])
        ohs = at("ohs", 199.5, [33, TW])
        line = at("line", 202.5, [NH, TW - 128])
        line2 = at("line2", 198.75, [NH, 128])
        hid = at("hid", 202.5, [P, 8, 64])
        gel = [hid[:, 6, :], hid[:, 4, :]]
        kcn = at("kcn", 4.25, [P, 32])

        bank = [ctx.enter_context(nc.psum_tensor(f"bank{n}", [P, 512], F32)) for n in range(8)]

        w_landed = [sem(f"w_landed{n}") for n in range(NRAW)]
        w_split = sem("w_split")
        w_open = sem("w_open")
        w_hi = sem("w_hi")
        w_used = sem("w_used")
        x_in = [sem(f"x_in{n}") for n in range(4)]
        consts_in = sem("consts_in")
        bias_line = sem("bias_line")
        line_out = sem("line_out")
        skew_out = sem("skew_out")
        bias_in = sem("bias_in")
        x_again = sem("x_again")
        set_up = sem("set_up")
        lines_copied = sem("lines_copied")
        y_read = sem("y_read")
        gs_raw = sem("gs_raw")
        free = [sem("bank0_read"), sem("bank1_read")]
        stat_in = sem("stat_in")
        stat_out = sem("stat_out")
        rs_ready = sem("rs_ready")
        rs_used = sem("rs_used")
        act_step = sem("act_step")
        dve_step = sem("dve_step")
        hf_ready, h_hi, h_lo = sem("hf_ready"), sem("h_hi"), sem("h_lo")
        f_exp, q_copied, kq_ready = sem("f_exp"), sem("q_copied"), sem("kq_ready")
        decayed = sem("decayed")
        sc_done = sem("sc_done")
        sc_kept = [sem("sc_kept6"), sem("sc_kept7")]
        tok_copied = sem("tok_copied")
        o_done = sem("o_done")
        o_free = sem("o_free")
        g_sig = sem("g_sig")
        gs_ready = sem("gs_ready")
        raw_copied = sem("raw_copied")
        normed = sem("normed")
        oa_f, oa_hi, oa_lo = sem("oa_f"), sem("oa_hi"), sem("oa_lo")
        xc_f, xc_hi, xc_lo = sem("xc_f"), sem("xc_hi"), sem("xc_lo")
        cexp, csum = sem("cexp"), sem("csum")
        gel_ready, cmp_out, kcn_ready, vbd_ready = (sem(n) for n in ("gel_ready", "cmp_out", "kcn_ready", "vbd_ready"))
        cs_done, cs_shift, cp_ready, cpT_done, cpT_copied, co_done, co_kept = (
            sem(n) for n in ("cs_done", "cs_shift", "cp_ready", "cpT_done", "cpT_copied", "co_done", "co_kept"))
        s_done, s_shift, p_ready, t_done = (sem(n) for n in ("s_done", "s_shift", "p_ready", "t_done"))
        pt_ready = [sem("pt_ready_s"), sem("pt_ready_w")]
        pv_done, ob_read, ot_ready, ot_done, ob_hi, ob_lo = (
            sem(n) for n in ("pv_done", "ob_read", "ot_ready", "ot_done", "ob_hi", "ob_lo"))
        gate_sig = sem("gate_sig")
        mix_f, mix_hi, mix_lo = sem("mix_f"), sem("mix_hi"), sem("mix_lo")
        x2_ready, x2_sq, sq_sum = sem("x2_ready"), sem("x2_sq"), sem("sq_sum")
        relu_d, u_t, u_f, u_hi, u_lo = (sem(n) for n in ("relu_d", "u_t", "u_f", "u_hi", "u_lo"))
        y_ready, y_out = sem("y_ready"), sem("y_out")

        users = []
        for h in range(HG):
            users += [f"f{h}", f"q{h}"]
        users = ["stat_x"] + users + ["kc", "vc", "ks", "kw", "st_ks", "nq0", "st_kw", "nq1", "st_q0", "nq2", "st_q1",
                 "nq3", "st_q2", "st_q3", "g0", "g1", "cmp_k", "g2", "st_kc", "g3", "cmp_v"]
        for h in range(HG):
            users += [f"ga{h}", f"st_o{h}"]
        users += ["ga4", "ga5", "ga6", "ga7", "gb0", "gb1", "gb2"]

        units = []
        for qb in range(ST):
            nh = 4 // (qb + 1) if qb < 2 else 1
            units += [(qb, list(range(h, h + nh)), b) for h in range(0, NH, nh) for b in range(2)]
        NU = len(units)
        first_unit = [min(u for u in range(NU) if units[u][0] == qb) for qb in range(ST)] + [NU]
        behind = {u: [] for u in range(NU)}
        for n, u in enumerate((3, 12, 21, 30, NU - 1)):
            behind[u].append(f"gb{3 + n}")
        for qb in range(1, ST):
            behind[first_unit[qb] + 2].append(f"oT{qb - 1}")
        behind[NU - 1].append(f"oT{ST - 1}")
        for u in range(NU):
            users += behind[u]
        users += [f"wo{n}" for n in range(KT)] + ["st_x2"]
        USE = {name: n for n, name in enumerate(users)}
        U0 = len(users)

        def bank_of(name):
            return bank[USE[name] % 2]

        block = ctx.enter_context(nc.Block())

        @block.sync
        def _(sp):
            def load(c, slot):
                sp.dma_start(wraw[:, slot, :], w[c]).then_inc(w_landed[slot], 16)

            for n in range(4):
                sp.dma_start(x0[:, 2 * n:2 * n + 2, :], xT[:, 2 * n:2 * n + 2, :]).then_inc(x_in[n], 16)
                if n >= 2:
                    load(n - 2, n - 2)
            for c in range(2, FIRST):
                if c >= NRAW:
                    sp.wait_ge(w_split, c - NRAW + 1)
                load(c, c % NRAW)
            with sp.Fori(0, (N_CHUNKS - FIRST) // 4) as i:
                for j in range(4):
                    sp.wait_ge(w_split, 4 * i + (FIRST + j - NRAW + 1))
                    load(4 * i + (FIRST + j), (FIRST + j) % NRAW)

        @block.gpsimd
        def _(pool):
            def split(c, raw, two):
                pool.tensor_scalar(whi[:, two, :], wraw[:, raw, :], 1.0, 0.0, ALU.mult, ALU.add).then_inc(w_hi, 1)
                pool.wait_ge(w_hi, c + 1)
                pool.tensor_tensor(wlo[:, two, :], wraw[:, raw, :], whi[:, two, :].bitcast(F32),
                                   ALU.subtract).then_inc(w_split, 1)

            for c in range(FIRST):
                pool.wait_ge(w_landed[c % NRAW], 16 * (c // NRAW + 1))
                if c >= NSPLIT:
                    pool.wait_ge(w_used, c - NSPLIT + 1)
                split(c, c % NRAW, c % NSPLIT)
            with pool.Fori(0, (N_CHUNKS - FIRST) // 4) as i:
                for j in range(4):
                    c = FIRST + j
                    pool.wait_ge(w_landed[c % NRAW], 16 * i + 16 * (c // NRAW + 1))
                    pool.wait_ge(w_used, 4 * i + (c - NSPLIT + 1))
                    pool.sem_inc(w_open, 1)
                    split(4 * i + c, c % NRAW, c % NSPLIT)

        @block.tensor
        def _(pe):
            def take(name):
                c = AT[name]
                pe.wait_ge(w_split, c + 1)
                return whi[:, c % NSPLIT, :], wlo[:, c % NSPLIT, :]

            def claim(name):
                n = USE[name]
                if n >= 2:
                    pe.wait_ge(free[n % 2], n // 2)
                return bank[n % 2]

            def three(out_, wh, wl, mh, ml, first, last):
                pe.matmul(out_, wh, mh, start=first, stop=False)
                pe.matmul(out_, wh, ml, start=False, stop=False)
                return pe.matmul(out_, wl, mh, start=False, stop=last)

            def project(name, hi=None, lo=None, each_k=None):
                hi = hhi if hi is None else hi
                lo = hlo if lo is None else lo
                wh, wl = take(name)
                to = claim(name)
                for k in range(KT):
                    if each_k is not None:
                        each_k(k)
                    c = slice(k * P, k * P + P)
                    last = three(to[:], wh[:, c], wl[:, c], hi[:, k, :], lo[:, k, :], k == 0, k == KT - 1)
                last.then_inc(w_used, 1)

            stats = [0]

            def stat(name, matrix, squares, n=S):
                stats[0] += 1
                pe.wait_ge(stat_in, stats[0])
                to = claim(name)
                pe.matmul(to[:, 0:n], matrix, squares, start=True, stop=True).then_inc(stat_out, 1)

            pe.wait_ge(set_up, 3)
            stat("stat_x", ones[:], xsq[:, 0, :])
            pe.wait_ge(consts_in, 16 * N_CONSTS)
            pe.matmul(bank[2][0:NH, 0:512], relx[:], ohs[:, 0:512], start=True, stop=True).then_inc(bias_line, 1)
            pe.matmul(bank[3][0:NH, 0:P], relx[:], ohs[:, 512:TW], start=True, stop=True).then_inc(bias_line, 1)

            def h_split(k):
                pe.wait_ge(h_lo, k + 1)

            for h in range(HG):
                project(f"f{h}", each_k=h_split if h == 0 else None)
                project(f"q{h}")

            def token_major(names, tiles, cols):
                k = 0
                for name, nk in zip(names, tiles):
                    wh, wl = take(name)
                    for kk in range(nk):
                        c = slice(kk * cols, kk * cols + cols)
                        for t in range(ST):
                            to = bank[2 + t][:, 0:cols]
                            hh, hl = hhi[:, k, t * P:t * P + P], hlo[:, k, t * P:t * P + P]
                            pe.matmul(to, hh, wh[:, c], start=k == 0, stop=False)
                            pe.matmul(to, hh, wl[:, c], start=False, stop=False)
                            last = pe.matmul(to, hl, wh[:, c], start=False, stop=k == KT - 1)
                        k += 1
                    last.then_inc(w_used, 1)
                    yield

            pe.wait_ge(lines_copied, 2)
            for _ in token_major([f"i{c}" for c in range(4)], [2] * 4, 512):
                pass

            sc_banks = [0]

            def sc_bank():
                n = sc_banks[0]
                if n >= 2:
                    pe.wait_ge(sc_kept[n % 2], n // 2)
                sc_banks[0] += 1
                return bank[6 + n % 2]

            def own(hs):
                for h in hs:
                    pe.wait_ge(kq_ready, h + 1)
                    to = sc_bank()
                    for t in range(ST):
                        c = slice(t * P, t * P + P)
                        last = pe.matmul(to[:, c], k_dec[:, h, c], q_raw[:, h, c], start=True, stop=True)
                    last.then_inc(sc_done, 1)

            def level(n):
                m = LEVELS[n]
                pe.wait_ge(decayed, n + 1)
                for pair in range(2):
                    to = sc_bank()
                    for h in (2 * pair, 2 * pair + 1):
                        for t in range(ST):
                            right = q_dec[:, h, t * P:t * P + P].rearrange("p (n two m) -> p n two m", two=2, m=m)
                            c = (h % 2) * 256 + t * 64
                            last = pe.matmul(to[:, c:c + 64].rearrange("p (n m) -> p n m", m=m),
                                             k_dec[:, h, t * P:t * P + P], right[:, :, 1, :], start=True, stop=True)
                    last.then_inc(sc_done, 1)

            def level_128():
                pe.wait_ge(decayed, 8)
                for pair in range(2):
                    to = sc_bank()
                    for h in (2 * pair, 2 * pair + 1):
                        for j in range(2):
                            c = (h % 2) * 256 + j * P
                            last = pe.matmul(to[:, c:c + P], k_dec[:, h, 2 * j * P:2 * j * P + P],
                                             q_dec[:, h, (2 * j + 1) * P:(2 * j + 2) * P], start=True, stop=True)
                    last.then_inc(sc_done, 1)

            def level_256(hs):
                pe.wait_ge(decayed, 9)
                for h in hs:
                    to = sc_bank()
                    for j in range(2):
                        last = pe.matmul(to[:, 256 * j:256 * j + 256], k_dec[:, h, j * P:j * P + P],
                                         q_dec[:, h, 256:512], start=True, stop=True)
                    last.then_inc(sc_done, 1)

            project("kc")
            own((0, 1))
            project("vc")
            own((2, 3))
            project("ks")
            level(0)
            project("kw")
            stat("st_ks", pair_ones[:], sq[:, 0, :])
            level(1)
            project("nq0")
            stat("st_kw", pair_ones[:], sq[:, 1, :])
            level(2)
            project("nq1")
            stat("st_q0", pair_ones[:], sq[:, 0, :])
            level(3)
            project("nq2")
            stat("st_q1", pair_ones[:], sq[:, 1, :])
            level(4)
            project("nq3")
            stat("st_q2", pair_ones[:], sq[:, 0, :])
            level(5)
            pe.wait_ge(tok_copied, 4)
            parts = token_major(["m0", "m1", "m2"], NM, MCOLS)
            next(parts)
            stat("st_q3", pair_ones[:], sq[:, 1, :])
            level(6)
            next(parts)
            level_128()
            next(parts)
            for _ in parts:
                pass

            def hidden(j, half):
                pe.wait_ge(xc_lo, j + 1)
                wh, wl = take(f"c{j}{half}")
                for i in range(8):
                    n, c = 8 * half + i, slice(i * P, i * P + P)
                    last = three(bank[4 + j][:, 0:64], wh[:, c], wl[:, c], xhi[j][:, n].rearrange("p g c -> p (g c)"),
                                 xlo[j][:, n].rearrange("p g c -> p (g c)"), n == 0, n == 15)
                last.then_inc(w_used, 1)

            pe.wait_ge(tok_copied, 8)
            hidden(0, 0)
            project("g0")
            level_256((0, 1))
            hidden(0, 1)
            project("g1")
            level_256((2, 3))
            hidden(1, 0)
            pe.wait_ge(gel_ready, 1)
            to = claim("cmp_k")
            pe.matmul(to[:, 0:64], w2_k, gel[0], start=True, stop=True).then_inc(cmp_out, 1)
            project("g2")
            hidden(1, 1)
            stat("st_kc", pair_ones[:], hid[:, 7, :], 64)

            for n in range(2):
                pe.wait_ge(sc_kept[n], 12)

            def mixed_values(h):
                to = bank[2 + h]
                for n, (s_t, t0, blk, nb) in enumerate(
                        [(0, 0, 0, 1), (0, 1, 4, 1), (0, 2, 6, 2), (1, 1, 1, 1), (1, 2, 8, 2), (2, 2, 2, 1),
                         (2, 3, 5, 1), (3, 3, 3, 1)]):
                    last = pe.matmul(to[:, t0 * P:(t0 + nb) * P], v_i[:, s_t, h * P:h * P + P],
                                     sc[:, h, blk:blk + nb, :].rearrange("p b t -> p (b t)"),
                                     start=n == 0, stop=n == 7, skip_group_check=True)
                last.then_inc(o_done, 1)

            mixed_values(0)
            mixed_values(1)
            project("g3")
            pe.wait_ge(csum, 2)
            mixed_values(2)
            mixed_values(3)
            pe.wait_ge(gel_ready, 2)
            to = claim("cmp_v")
            for g in range(2):
                for j in range(4):
                    last = pe.matmul(to[32 * j:32 * j + 32, g * 64:g * 64 + 64], gel[1][:, g * 32:g * 32 + 32],
                                     w2_v, start=True, stop=True, skip_group_check=True)
            last.then_inc(cmp_out, 1)
            for h in range(HG):
                project(f"ga{h}")
                stat(f"st_o{h}", ones[:], sq[:, h % 2, :])

            def q_tile(h, qb):
                g, i = divmod(h, 4)
                return qn[64 * g:64 * g + 64, i, qb * P:qb * P + P], slice(64 * g, 64 * g + 64)

            project("ga4")
            pe.wait_ge(normed, 6)
            pe.wait_ge(kcn_ready, 1)
            pe.wait_ge(o_free, 4)

            def c_scores(qb):
                if qb:
                    pe.wait_ge(cs_shift, qb)
                for h in range(NH):
                    q_, rows = q_tile(h, qb)
                    g, i = divmod(h, 4)
                    last = pe.matmul(bank[2 + g][:, 32 * i:32 * i + NCMP], q_, kcn[rows, 0:NCMP], start=True, stop=True)
                last.then_inc(cs_done, 1)

            def c_turn(qb):
                pe.wait_ge(cp_ready, qb + 1)
                for g in range(2):
                    last = pe.transpose(bank[4][:, g * P:g * P + P], pc[:, g * P:g * P + P], ident[:])
                last.then_inc(cpT_done, 1)

            def c_values(qb):
                pe.wait_ge(cpT_copied, qb + 1)
                pe.wait_ge(vbd_ready, 1)
                if qb:
                    pe.wait_ge(co_kept, qb)
                for g in range(2):
                    last = pe.matmul(bank[6][:, g * 256:g * 256 + 256], pcT[:, g, :], vbd[:, g, :],
                                     start=True, stop=True)
                last.then_inc(co_done, 1)

            c_scores(0)
            for qb, name in enumerate(("ga5", "ga6", "ga7", "gb0")):
                project(name)
                if qb:
                    c_values(qb - 1)
                c_turn(qb)
                if qb < ST - 1:
                    c_scores(qb + 1)
            project("gb1")
            c_values(ST - 1)

            keys = (ksn, kwn)

            def scores(u):
                qb, hs, b = units[u]
                n = (qb + 1) * P
                if u >= 2:
                    pe.wait_ge(s_shift, u - 1)
                for j, h in enumerate(hs):
                    q_, rows = q_tile(h, qb)
                    last = pe.matmul(bank[2 + u % 2][:, j * n:j * n + n], q_, keys[b][rows, 0:n],
                                     start=True, stop=True)
                last.then_inc(s_done, 1)

            def turn(u):
                qb, hs, b = units[u]
                pe.wait_ge(p_ready, u + 1)
                if u >= 2:
                    pe.wait_ge(pt_ready[b], u // 2)
                for kb in range(len(hs) * (qb + 1)):
                    last = pe.transpose(bank[4 + b][:, kb * P:kb * P + P], p_ring[:, u % 4, kb * P:kb * P + P],
                                        ident[:])
                last.then_inc(t_done, 1)

            def values(u):
                qb, hs, b = units[u]
                pe.wait_ge(pt_ready[b], u // 2 + 1)
                if qb and u == first_unit[qb]:
                    pe.wait_ge(ob_read, 2 * qb)
                for j, h in enumerate(hs):
                    g = h // 4
                    for kb in range(qb + 1):
                        c = (j * (qb + 1) + kb) * P
                        last = pe.matmul(bank[6 + b][:, h * 64:h * 64 + 64], pT[:, u % 3, c:c + P],
                                         v_sw[:, kb, b * P + g * 64:b * P + g * 64 + 64],
                                         start=kb == 0, stop=kb == qb)
                last.then_inc(pv_done, 1)

            def turn_out(qb):
                pe.wait_ge(ot_ready, qb + 1)
                to = claim(f"oT{qb}")
                for i in range(4):
                    last = pe.transpose(to[:, i * P:i * P + P], o_tok[:, qb, i * P:i * P + P], ident[:])
                last.then_inc(ot_done, 1)

            for u in range(NU + LAG_V):
                if u < NU:
                    scores(u)
                if u == 1:
                    project("gb2")
                if LAG_T <= u < NU + LAG_T:
                    turn(u - LAG_T)
                if u == LAG_V:
                    pe.wait_ge(co_kept, ST)
                if u >= LAG_V:
                    values(u - LAG_V)
                    for name in behind[u - LAG_V]:
                        if name[0] == "g":
                            project(name)
                        else:
                            turn_out(int(name[2]))

            pe.wait_ge(oa_lo, HG)
            pe.wait_ge(pt_ready[0], NU // 2)
            pe.wait_ge(pt_ready[1], NU // 2)
            for n in range(KT):
                wh, wl = take(f"ab{n}")
                for j, (hi, lo) in enumerate(((oahi, oalo), (obhi, oblo))):
                    if n == 0 and j == 1:
                        pe.wait_ge(ob_lo, ST)
                    if n >= 2:
                        pe.wait_ge(y_read, 2 * (n - 2) + j + 1)
                    to = bank[2 + (2 * n + j) % 4]
                    for k in range(4):
                        c = slice((4 * j + k) * P, (4 * j + k + 1) * P)
                        last = three(to[:], wh[:, c], wl[:, c], hi[:, k, :], lo[:, k, :], k == 0, k == 3)
                last.then_inc(w_used, 1)

            def mix_split(k):
                pe.wait_ge(mix_lo, k + 1)

            for n in range(KT):
                project(f"wo{n}", each_k=mix_split if n == 0 else None)
            stat("st_x2", ones[:], tmp[:])

            for half in range(HALVES):
                c0 = N_STRAIGHT + half * 2 * UP_T
                r0 = U0 + half * (UP_T + KT)
                with pe.Fori(0, UP_T // 4) as i:
                    for j in range(4):
                        slot, b = (c0 + j) % NSPLIT, (r0 + j) % 2
                        pe.wait_ge(w_split, 4 * i + (c0 + j + 1))
                        pe.wait_ge(free[b], 2 * i + (r0 + j) // 2)
                        for k in range(KT):
                            if half == 0 and j == 0:
                                pe.wait_ge(h_lo, KT + k + 1)
                            c = slice(k * P, k * P + P)
                            last = three(bank[b][:], whi[:, slot, c], wlo[:, slot, c], ghi[:, k, :], glo[:, k, :],
                                         k == 0, k == KT - 1)
                        last.then_inc(w_used, 1)
                c0 += UP_T
                r0 += UP_T
                with pe.Fori(0, KT // 2) as i:
                    for j in range(2):
                        b = (r0 + j) % 2
                        pe.wait_ge(free[b], i + (r0 + j) // 2)
                        for part in range(2):
                            slot = (c0 + 2 * j + part) % NSPLIT
                            pe.wait_ge(w_split, 4 * i + (c0 + 2 * j + part + 1))
                            for k in range(8):
                                kk = 8 * part + k
                                if j == 0:
                                    pe.wait_ge(u_lo, half * UP_T + kk + 1)
                                c = slice(k * P, k * P + P)
                                last = three(bank[b][:], whi[:, slot, c], wlo[:, slot, c], uhi[:, kk, :],
                                             ulo[:, kk, :], kk == 0, kk == 15)
                            last.then_inc(w_used, 1)

        @block.scalar
        def _(act):
            for dst, src in ((small[:, 0:SMALL], small_in), (relx[0:32, :], rel), (ohs[:], oh),
                             (ident[:], ident_in), (cst[:, 168:360], w2), (mask_f[:], masks)):
                act.dma_start(dst, src).then_inc(consts_in, 16)
            act.preload_act_table_set("natural_log_exp_and_others")

            steps = [0]

            def link(ins):
                steps[0] += 1
                ins.then_inc(act_step, 1)
                act.wait_ge(act_step, steps[0])

            rs = [0]
            outs = [0]

            def inverse_rms(name, dim, n=S):
                outs[0] += 1
                act.wait_ge(stat_out, outs[0])
                to = rstd[:, rs[0] % 2, 0:n]
                if rs[0] >= 2:
                    act.wait_ge(rs_used, rs[0] - 1)
                link(act.activation(to, bank_of(name)[:, 0:n], ACT.Ln, scale=1.0 / dim, bias=eps))
                act.activation(to, to, ACT.Exp, scale=-0.5).then_inc(rs_ready, 1)
                rs[0] += 1
                return to

            def leave(ins, name):
                ins.then_inc(free[USE[name] % 2], 1)

            for n in range(4):
                act.wait_ge(x_in[n], 16)
                act.activation(xsq[:, 2 * n:2 * n + 2, :], x0[:, 2 * n:2 * n + 2, :], ACT.Square).then_inc(x2_sq, 1)
            act.wait_ge(set_up, 3)
            inverse_rms("stat_x", D)
            for k in range(KT):
                act.wait_ge(hf_ready, k + 1)
                act.activation(hhi[:, k, :], hf[:, k % 2, :], ACT.Copy).then_inc(h_hi, 1)

            act.wait_ge(bias_line, 2)
            act.activation(line[:], bank[2][0:NH, 0:512], ACT.Copy, scale=-1.0).then_inc(lines_copied, 1)
            act.activation(line2[:], bank[3][0:NH, 0:P], ACT.Copy, scale=-1.0).then_inc(lines_copied, 1)
            act.wait_ge(lines_copied, 2)
            act.dma_start(scratch[:, 0:512], line[:]).then_inc(line_out, 16)
            act.dma_start(scratch[:, 512:TW], line2[:]).then_inc(line_out, 16)

            for h in range(HG):
                act.wait_ge(w_used, AT[f"f{h}"] + 1)
                if h == 0:
                    act.wait_ge(h_lo, KT)
                link(act.activation(e[:, h, :], bank_of(f"f{h}")[:], ACT.Exp, scale=-1.0))
                act.sem_inc(free[USE[f"f{h}"] % 2], 1)
                act.sem_inc(f_exp, 1)
                act.wait_ge(w_used, AT[f"q{h}"] + 1)
                link(act.activation(q_raw[:, h, :], bank_of(f"q{h}")[:], ACT.Copy))
                act.sem_inc(free[USE[f"q{h}"] % 2], 1)
                act.sem_inc(q_copied, 1)
            act.wait_ge(line_out, 32)
            act.dma_start(skewed, bass.AP(tensor=scratch.tensor, offset=P - 1, ap=[[TW, NH], [-1, P], [1, S]])
                          ).then_inc(skew_out, 16)
            act.wait_ge(w_used, AT["i3"] + 1)
            for t in range(ST):
                act.activation(v_i[:, t, :], bank[2 + t][:], ACT.Copy).then_inc(tok_copied, 1)

            squares = [0]

            def raw_and_square(name, raw):
                act.wait_ge(w_used, AT[name] + 1)
                act.activation(raw, bank_of(name)[:], ACT.Copy).then_inc(raw_copied, 1)
                if squares[0] >= 2:
                    act.wait_ge(stat_out, squares[0])
                link(act.activation(sq[:, squares[0] % 2, :], bank_of(name)[:], ACT.Square))
                act.sem_inc(free[USE[name] % 2], 1)
                act.sem_inc(stat_in, 1)
                squares[0] += 1

            raw_and_square("ks", ksn[:])
            raw_and_square("kw", kwn[:])
            inverse_rms("st_ks", DH)
            raw_and_square("nq0", qn[:, 0, :])
            inverse_rms("st_kw", DH)
            raw_and_square("nq1", qn[:, 1, :])
            inverse_rms("st_q0", DH)
            def block_high(j):
                act.wait_ge(xc_f, j + 1)
                act.activation(xhi[j][:], xf[j][:], ACT.Copy).then_inc(xc_hi, 1)

            raw_and_square("nq2", qn[:, 2, :])
            inverse_rms("st_q1", DH)
            block_high(0)
            raw_and_square("nq3", qn[:, 3, :])
            inverse_rms("st_q2", DH)
            block_high(1)
            inverse_rms("st_q3", DH)
            for n in range(2):
                act.wait_ge(sc_done, 4 + 14 + n + 1)
                act.activation(sc[:, 2 * n:2 * n + 2, 4:6, :].rearrange("p h b t -> p h (b t)"),
                               bank[6 + n][:].rearrange("p (h t) -> p h t", h=2), ACT.Copy).then_inc(sc_kept[n], 1)
            act.wait_ge(w_used, AT["m2"] + 1)
            for t in range(ST):
                act.activation(v_sw[:, t, :], bank[2 + t][:, 0:256], ACT.Copy)
                act.activation(gate3[:, t, :], bank[2 + t][:, 256:MCOLS], ACT.Exp, scale=-1.0).then_inc(tok_copied, 1)

            def gelu_exp(j):
                act.wait_ge(csum, j + 1)
                act.activation(hid[:, 3 * j + 2, :], hid[:, 3 * j + 1, :], ACT.Exp,
                               scale=-2.0 * 0.7978845608028654).then_inc(cexp, 1)

            def copy_g(h):
                name = f"g{h}"
                act.wait_ge(w_used, AT[name] + 1)
                link(act.activation(gs[:, h, :], bank_of(name)[:], ACT.Copy))
                act.sem_inc(free[USE[name] % 2], 1)

            def copy_256(h):
                act.wait_ge(sc_done, 4 + 16 + h + 1)
                act.activation(sc[:, h, 6:10, :].rearrange("p b t -> p (b t)"), bank[6 + h % 2][:],
                               ACT.Copy).then_inc(sc_kept[h % 2], 1)

            def copy_gate(name):
                act.wait_ge(w_used, AT[name] + 1)
                act.activation(gates[:, "ab".index(name[1]), int(name[2]), :], bank_of(name)[:], ACT.Copy
                               ).then_inc(free[USE[name] % 2], 1)

            copy_g(0)
            copy_256(0)
            copy_256(1)
            gelu_exp(0)
            copy_g(1)
            copy_256(2)
            copy_256(3)
            act.wait_ge(cmp_out, 1)
            link(act.activation(hid[:, 0, :], bank_of("cmp_k")[:, 0:64], ACT.Copy))
            link(act.activation(hid[:, 7, :], bank_of("cmp_k")[:, 0:64], ACT.Square))
            act.sem_inc(free[USE["cmp_k"] % 2], 1)
            act.sem_inc(stat_in, 1)
            copy_g(2)
            inverse_rms("st_kc", DH, 64)
            gelu_exp(1)

            def square_o(h):
                act.wait_ge(o_done, h + 1)
                act.wait_ge(stat_out, 7 if h < 2 else 7 + h)
                act.activation(sq[:, h % 2, :], bank[2 + h][:], ACT.Square).then_inc(stat_in, 1)

            square_o(0)
            square_o(1)
            copy_g(3)
            act.wait_ge(decayed, 9)
            act.activation(e[:], gs[:], ACT.Sigmoid).then_inc(g_sig, 1)
            for h in range(HG):
                copy_gate(f"ga{h}")
                inverse_rms(f"st_o{h}", P)
                if h < 2:
                    square_o(h + 2)
                act.wait_ge(oa_f, h + 1)
                act.activation(oahi[:, h, :], o_ring[:, h % 2, :], ACT.Copy).then_inc(oa_hi, 1)
                if h == 0:
                    act.wait_ge(skew_out, 16)
                    act.dma_start(bias[:], skewed.rearrange("h p u -> p h u")).then_inc(bias_in, 16)

            copy_gate("ga4")
            for qb in range(ST):
                act.wait_ge(cs_shift, qb + 1)
                nc_ = 8 * qb + 7
                pcv = pc[:].rearrange("p (h c) -> p h c", h=NH)[:, :, 0:nc_]
                act.activation(pcv, pcv, ACT.Exp, scale=-1.0).then_inc(cp_ready, 1)
                copy_gate(("ga5", "ga6", "ga7", "gb0")[qb])
                act.wait_ge(cpT_done, qb + 1)
                if qb:
                    act.wait_ge(co_done, qb)
                act.activation(pcT[:].rearrange("p g t -> p (g t)"), bank[4][:, 0:256], ACT.Copy).then_inc(cpT_copied, 1)
            copy_gate("gb1")

            def evacuate(u):
                qb, hs, b = units[u]
                n = len(hs) * (qb + 1) * P
                act.wait_ge(t_done, u + 1)
                if u >= 3:
                    act.wait_ge(pv_done, u - 2)
                act.activation(pT[:, u % 3, 0:n], bank[4 + b][:, 0:n], ACT.Copy).then_inc(pt_ready[b], 1)

            def out_high(qb):
                act.wait_ge(ot_done, qb + 1)
                act.activation(obhi[:, :, qb * P:qb * P + P], bank_of(f"oT{qb}")[:].rearrange("p (i t) -> p i t", i=4),
                               ACT.Copy).then_inc(ob_hi, 1)

            for u in range(NU + LAG_V):
                if u < NU:
                    qb, hs, b = units[u]
                    n = (qb + 1) * P
                    act.wait_ge(s_shift, u + 1)
                    if qb >= 2 and u == first_unit[qb]:
                        act.wait_ge(ob_read, 2 * qb - 3)
                    for j, h in enumerate(hs):
                        p_ = p_ring[:, u % 4, j * n:j * n + n]
                        last = act.activation(p_, p_, ACT.Exp, scale=-1.0, bias=mins[:, u % 4, j:j + 1],
                                              accum_out=sums[qb % 2][:, b, h:h + 1])
                    last.then_inc(p_ready, 1)
                if u == 1:
                    copy_gate("gb2")
                if LAG_T <= u < NU + LAG_T and units[u - LAG_T][2] == 0:
                    evacuate(u - LAG_T)
                if u >= LAG_V:
                    for name in behind[u - LAG_V]:
                        if name[0] == "g":
                            copy_gate(name)
                        elif name != f"oT{ST - 1}":
                            out_high(int(name[2]))
            act.wait_ge(p_ready, NU)
            act.dma_start(x2[:], xT).then_inc(x_again, 16)
            out_high(ST - 1)

            for name in ("gb6", "gb7"):
                act.wait_ge(free[USE[name] % 2], USE[name] // 2 + 1)
            for n in range(4):
                g_ = gates[:, n % 2, 4 * (n // 2):4 * (n // 2) + 4, :]
                act.activation(g_, g_, ACT.Sigmoid).then_inc(gate_sig, 1)
            for n in range(KT):
                act.wait_ge(mix_f, n + 1)
                act.activation(hhi[:, n, :], rstd[:, n % 2, :], ACT.Copy).then_inc(mix_hi, 1)
            for n in range(KT):
                act.wait_ge(x2_ready, n + 1)
                act.activation(ghi[:, n, :], x2[:, n, :], ACT.Copy, scale=g_mlp[:, n:n + 1]).then_inc(h_hi, 1)
                if n >= 2:
                    act.wait_ge(sq_sum, n - 1)
                act.activation(sq[:, n % 2, :], x2[:, n, :], ACT.Square).then_inc(x2_sq, 1)
            outs[0] += 1
            act.wait_ge(stat_out, outs[0])
            link(act.activation(rstd[:, 0, :], bank_of("st_x2")[:], ACT.Ln, scale=1.0 / D, bias=eps))
            act.activation(rstd[:, 0, :], rstd[:, 0, :], ACT.Exp, scale=-1.0).then_inc(rs_ready, 1)

            for half in range(HALVES):
                c0 = N_STRAIGHT + half * 2 * UP_T
                r0 = U0 + half * (UP_T + KT)
                t0 = half * UP_T
                with act.Fori(0, UP_T // 4) as i:
                    for j in range(4):
                        b, s = (r0 + j) % 2, j % 2
                        act.wait_ge(w_used, 4 * i + (c0 + j + 1))
                        act.activation(r_ring[:, s, :], bank[b][:], ACT.Relu).then_inc(relu_d, 1)
                        act.wait_ge(u_f, 4 * i + (t0 + j + 1))
                        act.activation(uhi[:, 4 * i + j, :], u_ring[:, s, :], ACT.Copy).then_inc(u_hi, 1)
            for n in range(KT):
                act.wait_ge(y_ready, n + 1)
                act.dma_start(out[n], x2[:, n, :]).then_inc(y_out, 16)
            act.wait_ge(y_out, 16 * KT)

        @block.vector
        def _(dve):
            steps = [0]

            def link(ins):
                steps[0] += 1
                ins.then_inc(dve_step, 1)
                dve.wait_ge(dve_step, steps[0])

            def leave(ins, name):
                ins.then_inc(free[USE[name] % 2], 1)

            dve.memset(ones[:], 1.0).then_inc(set_up, 1)
            link(dve.memset(pair_ones[:], 0.0))
            dve.memset(pair_ones[0:64, 0:64], 1.0)
            dve.memset(eps, EPS)
            dve.memset(pair_ones[64:128, 64:128], 1.0).then_inc(set_up, 1)
            dve.memset(relx[32:33, :], -BIG).then_inc(set_up, 1)
            link(dve.memset(sc[:, :, 0:4, :], 0.0))

            for n in range(1, 4):
                dve.wait_ge(x2_sq, n + 1)
                link(dve.tensor_tensor(xsq[:, 0:2, :], xsq[:, 0:2, :], xsq[:, 2 * n:2 * n + 2, :], ALU.add))
            dve.tensor_tensor(xsq[:, 0, :], xsq[:, 0, :], xsq[:, 1, :], ALU.add).then_inc(stat_in, 1)
            dve.wait_ge(consts_in, 16 * N_CONSTS)

            def norm_to_h(x_, gain, rs_, ring, n0):
                for k in range(KT):
                    if k >= 2:
                        dve.wait_ge(h_lo, n0 + k - 1)
                    dve.scalar_tensor_tensor(ring[:, k % 2, :], x_[:, k, :], gain[:, k:k + 1], rs_, ALU.mult,
                                             ALU.mult).then_inc(hf_ready, 1)
                    if k >= 1:
                        low(k - 1, ring, n0)
                low(KT - 1, ring, n0)

            def low(k, ring, n0):
                dve.wait_ge(h_hi, n0 + k + 1)
                dve.tensor_tensor(hlo[:, k, :], ring[:, k % 2, :], hhi[:, k, :].bitcast(F32),
                                  ALU.subtract).then_inc(h_lo, 1)

            dve.wait_ge(rs_ready, 1)
            dve.sem_inc(free[USE["stat_x"] % 2], 1)
            norm_to_h(x0, g_mix, rstd[:, 0, :], hf, 0)
            dve.wait_ge(h_lo, KT)
            dve.sem_inc(rs_used, 1)
            link(dve.tensor_scalar(g_q, g_q, -(DH ** -0.5), None, ALU.mult))
            dve.tensor_copy(mask[:, 0:7 * 256].rearrange("p (l t c) -> p l t c", l=7, t=4),
                            mask_f[:, 0:7 * 64].rearrange("p (l one c) -> p l one c", l=7, one=1)
                            .broadcast_to([P, 7, 4, 64]))
            link(dve.tensor_copy(mask[:, 7 * 256:].rearrange("p (t c) -> p t c", t=4),
                                 mask_f[:, 7 * 64:].rearrange("p (one c) -> p one c", one=1)
                                 .broadcast_to([P, 4, P])))

            for h in range(HG):
                dve.wait_ge(f_exp, h + 1)
                link(dve.tensor_scalar(f[:, h, :], e[:, h, :], BIG, 1.0, ALU.min, ALU.add))
                link(dve.reciprocal(f[:, h, :], f[:, h, :]))
                link(dve.scalar_tensor_tensor(k_dec[:, h, :], e[:, h, :], BIG, f[:, h, :], ALU.min, ALU.mult))
                dve.wait_ge(q_copied, h + 1)
                dve.tensor_tensor(q_dec[:, h, :], q_raw[:, h, :], f[:, h, :], ALU.mult).then_inc(kq_ready, 1)
            dve.wait_ge(kq_ready, HG)
            dve.sem_inc(decayed, 1)

            def copy_raw(name, to):
                dve.wait_ge(w_used, AT[name] + 1)
                link(dve.tensor_copy(to, bank_of(name)[:]))
                dve.sem_inc(free[USE[name] % 2], 1)

            def keep_own(hs):
                for h in hs:
                    dve.wait_ge(sc_done, h + 1)
                    dve.copy_predicated(sc[:, h, 0:4, :].rearrange("p b t -> p (b t)"), mask[:, 7 * 256:],
                                        bank[6 + h % 2][:]).then_inc(sc_kept[h % 2], 1)

            tot_at = {}
            o_ = 0
            for m in LEVELS[1:]:
                tot_at[m] = (o_, HG * S // m)
                o_ += HG * S // m

            def totals(m):
                if m == 1:
                    return f[:].rearrange("p h t -> p (h t)")
                return tot[:, tot_at[m][0]:tot_at[m][0] + tot_at[m][1]]

            def advance(n):
                m = LEVELS[n]
                nb = HG * S // (2 * m)
                t = totals(m).rearrange("p (n two) -> p n two", two=2)
                kv = k_dec[:].rearrange("p h t -> p (h t)").rearrange("p (n two m) -> p n two m", two=2, m=m)
                qv = q_dec[:].rearrange("p h t -> p (h t)").rearrange("p (n two m) -> p n two m", two=2, m=m)
                dve.tensor_tensor(totals(2 * m).rearrange("p (n one) -> p n one", one=1), t[:, :, 0:1], t[:, :, 1:2],
                                  ALU.mult)
                dve.tensor_tensor(kv[:, :, 0, :], kv[:, :, 0, :], t[:, :, 1:2].broadcast_to([P, nb, m]), ALU.mult)
                link(dve.tensor_tensor(qv[:, :, 1, :], qv[:, :, 1, :], t[:, :, 0:1].broadcast_to([P, nb, m]),
                                       ALU.mult))
                dve.sem_inc(decayed, 1)

            def keep_level(n):
                m = LEVELS[n]
                for h in range(HG):
                    c = (h % 2) * 256
                    to = sc[:, h, 0:4, :].rearrange("p b t -> p (b t)").rearrange("p (n two m) -> p n two m",
                                                                                 two=2, m=m)
                    ins = dve.copy_predicated(to[:, :, 1, :],
                                              mask[:, n * 256:n * 256 + 256].rearrange("p (n m) -> p n m", m=m),
                                              bank[6 + h // 2][:, c:c + 256].rearrange("p (n m) -> p n m", m=m))
                    if h % 2:
                        ins.then_inc(sc_kept[h // 2], 1)

            normed_n = [0]

            def norm(raw, gain):
                n = normed_n[0]
                dve.wait_ge(rs_ready, n + 2)
                dve.wait_ge(raw_copied, n + 1)
                link(dve.scalar_tensor_tensor(raw, raw, gain, rstd[:, (n + 1) % 2, :], ALU.mult, ALU.mult))
                dve.sem_inc(rs_used, 1)
                dve.sem_inc(normed, 1)
                normed_n[0] += 1

            def leave_stat(name):
                dve.sem_inc(free[USE[name] % 2], 1)

            def blocks(j):
                raw, pos_ = ((kc_raw, pos_k), (vc_raw, pos_v))[j]
                for par in range(2):
                    for g in range(2):
                        v = raw[64 * g:64 * g + 64, :].rearrange("p (n b two) -> p b n two", b=8, two=2)
                        for a in range(2):
                            last = dve.tensor_copy(xf[j][64 * par:64 * par + 64, 8 * a:8 * a + 8, g, 0:NCMP],
                                                   v[:, :, a:a + NCMP, par])
                link(last)
                for g in range(2):
                    last = dve.tensor_tensor(xf[j][:, :, g, 0:NCMP], xf[j][:, :, g, 0:NCMP],
                                             pos_.rearrange("p (n one) -> p n one", one=1).broadcast_to([P, 16, NCMP]),
                                             ALU.add)
                link(last)
                dve.sem_inc(xc_f, 1)

            def blocks_low(j):
                dve.wait_ge(xc_hi, j + 1)
                dve.tensor_tensor(xlo[j][:], xf[j][:], xhi[j][:].bitcast(F32), ALU.subtract).then_inc(xc_lo, 1)

            for j in range(2):
                dve.memset(xf[j][:], 0.0)
            copy_raw("kc", kc_raw[:])
            keep_own((0, 1))
            copy_raw("vc", vc_raw[:])
            keep_own((2, 3))
            for n in range(7):
                dve.wait_ge(sc_done, 4 + 2 * n + 2)
                advance(n)
                keep_level(n)
                if n >= 1:
                    name, raw, gain = (("st_ks", ksn[:], g_ks), ("st_kw", kwn[:], g_kw), ("st_q0", qn[:, 0, :], g_q),
                                       ("st_q1", qn[:, 1, :], g_q), ("st_q2", qn[:, 2, :], g_q),
                                       ("st_q3", qn[:, 3, :], g_q))[n - 1]
                    norm(raw, gain)
                    leave_stat(name)
                if n in (1, 3):
                    blocks(n // 2)
                if n in (4, 5):
                    blocks_low(n - 4)
            dve.wait_ge(sc_done, 4 + 14 + 2)
            advance(7)
            dve.wait_ge(tok_copied, 8)
            link(dve.tensor_scalar(gate3, gate3, 1.0, None, ALU.add))
            link(dve.reciprocal(gate3, gate3))
            link(dve.memset(vbd[:], 0.0))
            for j in range(2):
                u_, t_, e_ = (hid[:, 3 * j + n, :] for n in range(3))
                dve.wait_ge(w_used, AT[f"c{j}1"] + 1)
                link(dve.tensor_scalar(u_, bank[4 + j][:, 0:64], (b1_k, b1_v)[j], None, ALU.add))
                link(dve.tensor_tensor(t_, u_, u_, ALU.mult))
                link(dve.tensor_scalar(t_, t_, 0.044715, 1.0, ALU.mult, ALU.add))
                link(dve.tensor_tensor(t_, t_, u_, ALU.mult))
                link(dve.tensor_scalar(t_, t_, -50.0, None, ALU.max))
                dve.sem_inc(csum, 1)
                dve.wait_ge(cexp, j + 1)
                link(dve.tensor_scalar(e_, e_, 1.0, None, ALU.add))
                link(dve.reciprocal(e_, e_))
                dve.tensor_tensor(gel[j], u_, e_, ALU.mult).then_inc(gel_ready, 1)
            dve.wait_ge(rs_ready, 8)
            leave_stat("st_kc")
            rs_ = rstd[:, 7 % 2, 0:64]
            for g in range(2):
                rows = slice(64 * g, 64 * g + 64)
                last = dve.scalar_tensor_tensor(kcn[rows, :], hid[rows, 0, 32 * g:32 * g + 32], g_kc[rows, :],
                                                rs_[rows, 32 * g:32 * g + 32], ALU.mult, ALU.mult)
            link(last)
            dve.sem_inc(rs_used, 1)
            dve.sem_inc(kcn_ready, 1)
            dve.wait_ge(g_sig, 1)
            link(dve.scalar_tensor_tensor(gs[:], gs[:], g_hg, e[:], ALU.mult, ALU.mult))
            dve.wait_ge(cmp_out, 2)
            for g in range(2):
                for j in range(4):
                    last = dve.tensor_copy(vbd[32 * j:32 * j + 32, g, 64 * j:64 * j + 64],
                                           bank_of("cmp_v")[32 * j:32 * j + 32, 64 * g:64 * g + 64])
            link(last)
            dve.sem_inc(vbd_ready, 1)
            leave_stat("cmp_v")

            def oa_low(h):
                dve.wait_ge(oa_hi, h + 1)
                dve.tensor_tensor(oalo[:, h, :], o_ring[:, h % 2, :], oahi[:, h, :].bitcast(F32),
                                  ALU.subtract).then_inc(oa_lo, 1)

            for h in range(HG):
                dve.wait_ge(rs_ready, 9 + h)
                leave_stat(f"st_o{h}")
                o_ = o_ring[:, h % 2, :]
                if h >= 2:
                    dve.wait_ge(oa_lo, h - 1)
                link(dve.tensor_tensor(o_, bank[2 + h][:], rstd[:, h % 2, :], ALU.mult))
                dve.sem_inc(rs_used, 1)
                dve.sem_inc(o_free, 1)
                dve.tensor_tensor(o_, o_, gs[:, h, :], ALU.mult).then_inc(oa_f, 1)
                if h:
                    oa_low(h - 1)
            oa_low(HG - 1)
            link(dve.memset(pc[:], 0.0))

            def by_head(v):
                return v.rearrange("p (h one) -> p h one", one=1)

            def c_shift(qb):
                nc_ = 8 * qb + 7
                dve.wait_ge(cs_done, qb + 1)
                if qb == 0:
                    dve.wait_ge(bias_in, 16)
                else:
                    dve.wait_ge(cpT_done, qb)
                pcv = pc[:].rearrange("p (h c) -> p h c", h=NH)[:, :, 0:nc_]
                s0 = 415 - 128 * qb
                for g in range(2):
                    hs = slice(4 * g, 4 * g + 4)
                    last = dve.tensor_tensor(
                        pcv[:, hs, :], bank[2 + g][:, 0:P].rearrange("p (h c) -> p h c", h=4)[:, :, 0:nc_],
                        bias[:, hs, s0:s0 + 16 * (nc_ - 1) + 1:16], ALU.add)
                link(last)
                link(dve.tensor_reduce(mc, pcv, AX_X, ALU.min))
                link(dve.tensor_tensor(pcv, pcv, by_head(mc).broadcast_to([P, NH, nc_]), ALU.subtract))
                dve.sem_inc(cs_shift, 1)
                dve.tensor_scalar(okc, mc, BIG / 10, None, ALU.is_lt)

            def c_weight(qb):
                nc_ = 8 * qb + 7
                pcv = pc[:].rearrange("p (h c) -> p h c", h=NH)[:, :, 0:nc_]
                wc = wcs[qb % 2]
                dve.wait_ge(cp_ready, qb + 1)
                link(dve.tensor_reduce(sumc, pcv, AX_X, ALU.add))
                link(dve.reciprocal(wc, sumc))
                link(dve.tensor_tensor(wc, wc, okc, ALU.mult))
                g3 = gate3[:, qb, :].rearrange("p (h c) -> p h c", c=3)
                link(dve.tensor_tensor(by_head(wc), by_head(wc), g3[:, :, 0:1], ALU.mult))

            def c_keep(qb):
                dve.wait_ge(co_done, qb + 1)
                dve.tensor_tensor(o_tok[:, qb, :].rearrange("p (h d) -> p h d", h=NH),
                                  bank[6][:].rearrange("p (h d) -> p h d", h=NH),
                                  by_head(wcs[qb % 2]).broadcast_to([P, NH, DH]), ALU.mult).then_inc(co_kept, 1)

            for qb in range(ST):
                c_shift(qb)
                if qb:
                    c_keep(qb - 1)
                c_weight(qb)

            def evacuate(u):
                qb, hs, b = units[u]
                n = len(hs) * (qb + 1) * P
                dve.wait_ge(t_done, u + 1)
                if u >= 3:
                    dve.wait_ge(pv_done, u - 2)
                dve.tensor_copy(pT[:, u % 3, 0:n], bank[4 + b][:, 0:n]).then_inc(pt_ready[b], 1)

            def weigh(qb):
                dve.wait_ge(p_ready, first_unit[qb + 1])
                link(dve.reciprocal(wts, sums[qb % 2]))
                dve.sem_inc(ob_read, 1)
                g3 = gate3[:, qb, :].rearrange("p (h c) -> p c h", c=3)
                link(dve.tensor_tensor(wts, wts, g3[:, 1:3, :], ALU.mult))
                dve.wait_ge(pv_done, first_unit[qb + 1])
                acc = o_tok[:, qb, :]
                for b in range(2):
                    link(dve.tensor_tensor(tmp[:].rearrange("p (h d) -> p h d", h=NH),
                                           bank[6 + b][:].rearrange("p (h d) -> p h d", h=NH),
                                           by_head(wts[:, b, :]).broadcast_to([P, NH, DH]), ALU.mult))
                    if b == 1:
                        dve.sem_inc(ob_read, 1)
                    link(dve.tensor_tensor(acc, acc, tmp[:], ALU.add))
                dve.sem_inc(ot_ready, 1)

            def out_low(qb):
                dve.wait_ge(ob_hi, qb + 1)
                c = slice(qb * P, qb * P + P)
                link(dve.tensor_tensor(oblo[:, :, c], bank_of(f"oT{qb}")[:].rearrange("p (i t) -> p i t", i=4),
                                       obhi[:, :, c].bitcast(F32), ALU.subtract))
                dve.sem_inc(ob_lo, 1)
                leave_stat(f"oT{qb}")

            for u in range(NU + LAG_V):
                if u < NU:
                    qb, hs, b = units[u]
                    n = (qb + 1) * P
                    dve.wait_ge(s_done, u + 1)
                    if u >= 4:
                        dve.wait_ge(t_done, u - 3)
                    for j, h in enumerate(hs):
                        last = dve.tensor_tensor_reduce(
                            out=p_ring[:, u % 4, j * n:j * n + n], in0=bank[2 + u % 2][:, j * n:j * n + n],
                            in1=bias[:, h, S - n:S], scale=1.0, scalar=3.0e38, op0=ALU.add,
                            op1=ALU.min, accum_out=mins[:, u % 4, j:j + 1])
                    last.then_inc(s_shift, 1)
                if u == 1:
                    c_keep(ST - 1)
                if LAG_T <= u < NU + LAG_T and units[u - LAG_T][2] == 1:
                    evacuate(u - LAG_T)
                if u >= LAG_V:
                    if u - LAG_V + 1 in first_unit[1:]:
                        weigh(units[u - LAG_V][0])
                    for name in behind[u - LAG_V]:
                        if name[0] == "o" and name != f"oT{ST - 1}":
                            out_low(int(name[2]))
            out_low(ST - 1)

            def mix_low(n):
                dve.wait_ge(mix_hi, n + 1)
                dve.tensor_tensor(hlo[:, n, :], rstd[:, n % 2, :], hhi[:, n, :].bitcast(F32),
                                  ALU.subtract).then_inc(mix_lo, 1)

            for n in range(KT):
                dve.wait_ge(gate_sig, 2 if n < 4 else 4)
                dve.wait_ge(w_used, AT[f"ab{n}"] + 1)
                if n >= 2:
                    dve.wait_ge(mix_lo, n - 1)
                for j in range(2):
                    dve.tensor_tensor(gates[:, j, n, :], gates[:, j, n, :], bank[2 + (2 * n + j) % 4][:],
                                      ALU.mult).then_inc(y_read, 1)
                dve.wait_ge(y_read, 2 * n + 2)
                dve.tensor_tensor(rstd[:, n % 2, :], gates[:, 0, n, :], gates[:, 1, n, :], ALU.add).then_inc(mix_f, 1)
                if n:
                    mix_low(n - 1)
            mix_low(KT - 1)
            dve.wait_ge(x_again, 16)
            def g_low(n):
                dve.wait_ge(h_hi, KT + n + 1)
                dve.scalar_tensor_tensor(glo[:, n, :], x2[:, n, :], g_mlp[:, n:n + 1], ghi[:, n, :].bitcast(F32),
                                         ALU.mult, ALU.subtract).then_inc(h_lo, 1)

            for n in range(KT):
                dve.wait_ge(w_used, AT[f"wo{n}"] + 1)
                link(dve.tensor_tensor(x2[:, n, :], x2[:, n, :], bank_of(f"wo{n}")[:], ALU.add))
                dve.sem_inc(x2_ready, 1)
                leave_stat(f"wo{n}")
                g_low(n)
                dve.wait_ge(x2_sq, 4 + n + 1)
                if n == 0:
                    link(dve.tensor_copy(tmp[:], sq[:, 0, :]))
                else:
                    link(dve.tensor_tensor(tmp[:], tmp[:], sq[:, n % 2, :], ALU.add))
                dve.sem_inc(sq_sum, 1)
            dve.sem_inc(stat_in, 1)
            dve.wait_ge(rs_ready, 13)
            leave_stat("st_x2")

            for half in range(HALVES):
                c0 = N_STRAIGHT + half * 2 * UP_T
                r0 = U0 + half * (UP_T + KT)
                t0 = half * UP_T
                with dve.Fori(0, UP_T // 4) as i:
                    for j in range(4):
                        b, s = (r0 + j) % 2, j % 2
                        dve.wait_ge(relu_d, 4 * i + (t0 + j + 1))
                        dve.tensor_tensor(t_ring[:, s, :], bank[b][:], rstd[:, 0, :], ALU.mult).then_inc(u_t, 1)
                        dve.wait_ge(u_t, 4 * i + (t0 + j + 1))
                        dve.tensor_tensor(u_ring[:, s, :], t_ring[:, s, :], r_ring[:, s, :], ALU.mult).then_inc(u_f, 1)
                        dve.wait_ge(u_hi, 4 * i + (t0 + j + 1))
                        dve.sem_inc(free[b], 1)
                        dve.tensor_tensor(ulo[:, 4 * i + j, :], u_ring[:, s, :], uhi[:, 4 * i + j, :].bitcast(F32),
                                          ALU.subtract).then_inc(u_lo, 1)
                c0 += UP_T
                r0 += UP_T
                with dve.Fori(0, KT // 2) as i:
                    for j in range(2):
                        b = (r0 + j) % 2
                        dve.wait_ge(w_used, 4 * i + (c0 + 2 * j + 2))
                        if half == 0:
                            dve.tensor_tensor(x2[:, 2 * i + j, :], x2[:, 2 * i + j, :], bank[b][:], ALU.add
                                              ).then_inc(free[b], 1)
                        else:
                            dve.tensor_tensor(x2[:, 2 * i + j, :], x2[:, 2 * i + j, :], bank[b][:], ALU.add
                                              ).then_inc(y_ready, 1)
                            dve.wait_ge(y_ready, 2 * i + (j + 1))
                            dve.sem_inc(free[b], 1)


def make_oh():
    dist = 511 - np.arange(TW)
    d = np.maximum(dist, 0)
    df = np.maximum(d, 1).astype(np.float32)
    large = 16 + (np.log(df / np.float32(16)) / np.float32(np.log(64.0)) * np.float32(16)).astype(np.int32)
    bucket = np.where(d < 16, d, np.minimum(large, 31))
    oh = np.zeros((33, TW), np.float32)
    oh[np.where(dist >= 0, bucket, 32), np.arange(TW)] = 1.0
    return oh


def make_masks():
    s = np.arange(P)[:, None]
    parts = []
    for m in LEVELS[:7]:
        n = np.arange(64)[None, :] // m
        parts.append((s // (2 * m) == n) & (s % (2 * m) < m))
    parts.append(np.eye(P, dtype=bool))
    return np.concatenate(parts, 1).astype(np.float32)


def lay_out(inputs):
    sizes = [512, 512, 512, 512, 512] + [128] * 6 + [24, 1024, 1024]
    offs = np.cumsum([0] + sizes)
    w_in = inputs["w_in"][0]
    hq, hf_, hi, hg, nq, kc, vc, ks, vs, kw, vw, ng, ga, gb = (
        w_in[:, offs[n]:offs[n + 1]] for n in range(14))

    def tiles(m):
        return m.reshape(-1, P, m.shape[1]).transpose(1, 0, 2).reshape(P, -1)

    w = np.zeros((N_CHUNKS, P, CW), np.float32)
    for h in range(4):
        c = slice(h * P, h * P + P)
        w[AT[f"f{h}"]] = tiles(hf_[:, c])
        w[AT[f"q{h}"]] = tiles(hq[:, c])
        w[AT[f"g{h}"]] = tiles(hg[:, c])
        w[AT[f"i{h}"]] = tiles(hi[256 * h:256 * h + 256])
        w[AT[f"nq{h}"]] = tiles(np.concatenate([nq[:, 64 * h:64 * h + 64], nq[:, 256 + 64 * h:320 + 64 * h]], 1))
    for name, m in (("kc", kc), ("vc", vc), ("ks", ks), ("kw", kw)):
        w[AT[name]] = tiles(m)
    m = np.concatenate([vs, vw, ng], 1)
    k = 0
    for n, nk in enumerate(NM):
        w[AT[f"m{n}"], :, 0:nk * MCOLS] = tiles(m[k * P:(k + nk) * P])
        k += nk
    w1 = inputs["cmp_w1"][0]
    for j in range(2):
        for half in range(2):
            w[AT[f"c{j}{half}"]] = tiles(w1[j, 1024 * half:1024 * half + 1024])
    wa, wb, wo = inputs["w_branch_a"][0], inputs["w_branch_b"][0], inputs["w_out"][0]
    for n in range(KT):
        c = slice(n * P, n * P + P)
        w[AT[f"ga{n}"]] = tiles(ga[:, c])
        w[AT[f"gb{n}"]] = tiles(gb[:, c])
        w[AT[f"ab{n}"], :, 0:512] = tiles(wa[:, c])
        w[AT[f"ab{n}"], :, 512:1024] = tiles(wb[:, c])
        w[AT[f"wo{n}"]] = tiles(wo[:, c])
    up, down = inputs["w_up"][0], inputs["w_down"][0]
    at = N_STRAIGHT
    for half in range(HALVES):
        for n in range(UP_T):
            c = (half * UP_T + n) * P
            w[at] = tiles(up[:, c:c + P])
            at += 1
        for n in range(KT):
            for part in range(2):
                r = (half * UP_T + 8 * part) * P
                w[at] = tiles(down[r:r + 1024, n * P:n * P + P])
                at += 1
    gqk = inputs["nsa_qk_gain"][0]
    pos = inputs["cmp_pos"][0].reshape(2, 16, 2, 64).transpose(2, 3, 0, 1).reshape(P, 32)
    w2 = inputs["cmp_w2"][0]
    return {
        "xT": inputs["x"][0].T.reshape(KT, P, S).transpose(1, 0, 2),
        "w": w,
        "oh": make_oh(),
        "masks": make_masks(),
        "ident_in": np.eye(P, dtype=np.float32),
        "small_in": np.concatenate([
            inputs["norm_mix"][0].reshape(KT, P).T, inputs["norm_mlp"][0].reshape(KT, P).T,
            inputs["hg_out_gain"][0].reshape(P, 1), np.concatenate([gqk.T, gqk.T], 0),
            inputs["cmp_b1"][0].T, pos], 1),
        "w2": np.concatenate([w2[0], w2[0], w2[1]], 1),
        "rel": inputs["rel_bias"],
    }


def kernel(**inputs):
    import concourse.bacc as bacc
    from concourse.bass_utils import run_bass_kernel_spmd

    nc = bacc.Bacc("TRN2", target_bir_lowering=False, num_devices=1)
    arrays = {f"in_{n}": np.ascontiguousarray(a) for n, a in lay_out(
        {n: np.asarray(a) for n, a in inputs.items()}).items()}
    aps = {n[3:]: nc.dram_tensor(n, a.shape, mybir.dt.from_np(a.dtype), kind="ExternalInput").ap()
           for n, a in arrays.items()}
    scratch = nc.dram_tensor("bias_lines", (NH, TW), F32, kind="Internal").ap()
    skewed = nc.dram_tensor("bias_skewed", (NH, P, S), F32, kind="Internal").ap()
    out = nc.dram_tensor("out", (KT, P, S), F32, kind="ExternalOutput").ap()
    build_block(nc, scratch=scratch, skewed=skewed, out=out, **aps)
    r = run_bass_kernel_spmd(nc, [arrays], core_ids=[0])
    return r.results[0]["out"].reshape(1, D, S).transpose(0, 2, 1)
```
